# Optimizing a Trainium2 kernel written in Bass

```python
import jax, jax.numpy as jnp
from jax import lax
import numpy as np

D_MODEL = 1024
BATCH = 1
SEQ = 2048
DEPTH = 1
DEC_BATCH = 8
DEC_SEQ = 8
PAST_LEN = 2048
PAGE_SIZE = 128

D_MIX = D_MODEL
D_A = D_MIX // 2
HEAD_DIM_A = 64
N_HEADS_A = D_A // HEAD_DIM_A
DILATED_CONFIGS = ((128, 1), (512, 4), (2048, 16))
WINDOW_MAX = 2048
ATTN_BLOCK = 128
ATTN_SCALE = HEAD_DIM_A ** -0.5
NUM_BUCKETS = 32
REL_MAX_DIST = 2048
D_B = D_MIX - D_A
N_HEADS_B = 4
HEAD_V_B = D_B // N_HEADS_B
EXPAND_B = 128
D_F = N_HEADS_B * EXPAND_B
GLA_CHUNK = 64
IN_WIDTHS = (D_A, D_A, D_A, D_A, D_F, D_F, D_B, D_B)
D_IN = sum(IN_WIDTHS)
IN_SPLITS = [int(s) for s in np.cumsum(IN_WIDTHS)[:-1]]
ALPHA = (2.0 * DEPTH) ** 0.25
BETA = (8.0 * DEPTH) ** -0.25
NORM_EPS = 1e-5

kernel_name = "hymba_dilated_hgrn2_deepnorm_step"

def _rel_buckets(dist):
    max_exact = NUM_BUCKETS // 2
    d = np.maximum(dist, 1).astype(np.float32)
    large = max_exact + (np.log(d / max_exact) / np.log(REL_MAX_DIST / max_exact)
                         * (NUM_BUCKETS - max_exact)).astype(np.int32)
    large = np.minimum(large, NUM_BUCKETS - 1)
    return np.where(dist < max_exact, dist, large).astype(np.int32)

def _rel_bias(table, dist):
    return jnp.moveaxis(table.astype(jnp.float32)[_rel_buckets(dist)], -1, 0)

def _attend(q, k, v, bias, mask):
    s = jnp.einsum('...qhd,...khd->...hqk', q.astype(jnp.float32), k.astype(jnp.float32)) * ATTN_SCALE + bias
    s = jnp.where(mask, s, -jnp.inf)
    m = jnp.max(s, axis=-1, keepdims=True)
    p = jnp.exp(s - m)
    den = jnp.sum(p, axis=-1, keepdims=True)
    out = jnp.einsum('...hqk,...khd->...qhd', p / den, v.astype(jnp.float32))
    lse = jnp.swapaxes((m + jnp.log(den))[..., 0], -1, -2)
    return out, lse

def _combine_by_denominator(outs, lses):
    w = jax.nn.softmax(jnp.stack(lses, axis=0), axis=0)
    return jnp.sum(w[..., None] * jnp.stack(outs, axis=0), axis=0)

def _dilated_prompt_cfg(q, k, v, rel_bias, window, dil):
    B, T, H, D = q.shape
    L = T // dil
    W = window // dil
    BQ = ATTN_BLOCK
    P = (-L) % BQ
    Lp = L + P
    nb = Lp // BQ

    def to_blocks(a):
        a = a.reshape(B, L, dil, H, D).transpose(0, 2, 1, 3, 4)
        a = jnp.pad(a, ((0, 0), (0, 0), (P, 0), (0, 0), (0, 0)))
        return a.reshape(B, dil, nb, BQ, H, D)

    def band(a):
        prev = jnp.pad(a, ((0, 0), (0, 0), (1, 0), (0, 0), (0, 0), (0, 0)))[:, :, :-1]
        return jnp.concatenate([prev, a], axis=3)

    qb = to_blocks(q)
    kb = band(to_blocks(k))
    vb = band(to_blocks(v))
    i = np.arange(BQ)[:, None]
    j = np.arange(2 * BQ)[None, :]
    sub = BQ + i - j
    band_ok = (sub >= 0) & (sub <= W)
    key_sub = (np.arange(nb)[:, None] - 1) * BQ + np.arange(2 * BQ)[None, :]
    q_sub = np.arange(nb)[:, None] * BQ + np.arange(BQ)[None, :]
    mask = band_ok[None] & ((key_sub >= P)[:, None, :] | (q_sub < P)[:, :, None])
    bias = _rel_bias(rel_bias, dil * np.clip(sub, 0, None))
    out, lse = _attend(qb, kb, vb, bias, mask[:, None])
    out = out.reshape(B, dil, Lp, H, D)[:, :, P:].transpose(0, 2, 1, 3, 4).reshape(B, T, H, D)
    lse = lse.reshape(B, dil, Lp, H)[:, :, P:].transpose(0, 2, 1, 3).reshape(B, T, H)
    return out, lse

def _dilated_sample_cfg(q, k_ext, v_ext, rel_bias, window, dil):
    B, Tn, H, D = q.shape
    Tk = k_ext.shape[1]
    W = window // dil
    idx = (Tk - Tn) + np.arange(Tn)[:, None] - dil * np.arange(W + 1)[None, :]
    valid = idx >= 0
    gidx = np.maximum(idx, 0)
    kg = k_ext[:, gidx]
    vg = v_ext[:, gidx]
    bias = _rel_bias(rel_bias, dil * np.arange(W + 1)[None, :])
    out, lse = _attend(q[:, :, None], kg, vg, bias, valid[:, None, None, :])
    return out[:, :, 0], lse[:, :, 0]

def _gla_chunked(q, k, v, g, S0, chunk):
    B, T, H, K = q.shape
    V = v.shape[-1]

    def chunks(a):
        return a.reshape(B, T // chunk, chunk, H, a.shape[-1]).transpose(1, 0, 3, 2, 4)

    causal = jnp.tril(jnp.ones((chunk, chunk), dtype=bool))

    def step(S, inp):
        qc, kc, vc, gc = inp
        b = jnp.cumsum(gc, axis=2)
        inter = jnp.einsum('bhck,bhkv->bhcv', qc * jnp.exp(b), S)
        diff = b[:, :, :, None, :] - b[:, :, None, :, :]
        decay = jnp.exp(jnp.where(causal[:, :, None], diff, -jnp.inf))
        A = jnp.einsum('bhtk,bhsk,bhtsk->bhts', qc, kc, decay)
        intra = jnp.einsum('bhts,bhsv->bhtv', A, vc)
        bC = b[:, :, -1]
        S_new = jnp.exp(bC)[..., None] * S + jnp.einsum(
            'bhsk,bhsv->bhkv', kc * jnp.exp(bC[:, :, None] - b), vc)
        return S_new, inter + intra

    S, o = lax.scan(step, S0, (chunks(q), chunks(k), chunks(v), chunks(g)))
    o = o.transpose(1, 0, 3, 2, 4).reshape(B, T, H, V)
    return o, S

def _hgrn2(qb, fb, ib, S0, lb, chunk):
    B, T, _ = qb.shape
    q = jax.nn.silu(qb.astype(jnp.float32)).reshape(B, T, N_HEADS_B, EXPAND_B) * EXPAND_B ** -0.5
    f = lb + (1.0 - lb) * jax.nn.sigmoid(fb.astype(jnp.float32))
    k = (1.0 - f).reshape(B, T, N_HEADS_B, EXPAND_B)
    g = jnp.log(f).reshape(B, T, N_HEADS_B, EXPAND_B)
    v = ib.astype(jnp.float32).reshape(B, T, N_HEADS_B, HEAD_V_B)
    return _gla_chunked(q, k, v, g, S0.astype(jnp.float32), chunk)

def _project(x, w_in):
    h = jnp.einsum('btd,de->bte', x, w_in)
    return jnp.split(h, IN_SPLITS, axis=-1)

def _heads_a(a):
    B, T, _ = a.shape
    return a.reshape(B, T, N_HEADS_A, HEAD_DIM_A)

def _merge(x, attn, ga, o_b, gb, w_out, norm_g, ln_g, ln_b):
    B, T, _ = x.shape
    a_out = attn.reshape(B, T, D_A).astype(x.dtype) * jax.nn.silu(ga)
    ms = jnp.mean(jnp.square(o_b), axis=-1, keepdims=True)
    o_n = o_b * lax.rsqrt(ms + NORM_EPS) * norm_g.astype(jnp.float32)
    b_out = o_n.reshape(B, T, D_B).astype(x.dtype) * jax.nn.silu(gb)
    mix = jnp.concatenate([a_out, b_out], axis=-1)
    z = (ALPHA * x + jnp.einsum('bte,ed->btd', mix, w_out)).astype(jnp.float32)
    mu = jnp.mean(z, axis=-1, keepdims=True)
    var = jnp.mean(jnp.square(z - mu), axis=-1, keepdims=True)
    y = (z - mu) * lax.rsqrt(var + NORM_EPS) * ln_g.astype(jnp.float32) + ln_b.astype(jnp.float32)
    return y.astype(x.dtype)

def _prompt_layer(x, w_in, w_out, rel_bias, lb, norm_g, ln_g, ln_b):
    B, T, _ = x.shape
    qa, ka, va, ga, qb, fb, ib, gb = _project(x, w_in)
    qa, ka, va = _heads_a(qa), _heads_a(ka), _heads_a(va)
    outs, lses = [], []
    for window, dil in DILATED_CONFIGS:
        o, l = _dilated_prompt_cfg(qa, ka, va, rel_bias, window, dil)
        outs.append(o)
        lses.append(l)
    attn = _combine_by_denominator(outs, lses)
    S0 = jnp.zeros((B, N_HEADS_B, EXPAND_B, HEAD_V_B), jnp.float32)
    o_b, S = _hgrn2(qb, fb, ib, S0, lb, min(GLA_CHUNK, T))
    y = _merge(x, attn, ga, o_b, gb, w_out, norm_g, ln_g, ln_b)
    keep = min(WINDOW_MAX, T)
    return y, ka[:, T - keep:], va[:, T - keep:], S

def _sample_layer(x, k_past, v_past, S0, w_in, w_out, rel_bias, lb, norm_g, ln_g, ln_b):
    B, T, _ = x.shape
    qa, ka, va, ga, qb, fb, ib, gb = _project(x, w_in)
    qa, ka, va = _heads_a(qa), _heads_a(ka), _heads_a(va)
    k_ext = jnp.concatenate([k_past, ka.astype(k_past.dtype)], axis=1)
    v_ext = jnp.concatenate([v_past, va.astype(v_past.dtype)], axis=1)
    outs, lses = [], []
    for window, dil in DILATED_CONFIGS:
        o, l = _dilated_sample_cfg(qa, k_ext, v_ext, rel_bias, window, dil)
        outs.append(o)
        lses.append(l)
    attn = _combine_by_denominator(outs, lses)
    o_b, S = _hgrn2(qb, fb, ib, S0, lb, T)
    y = _merge(x, attn, ga, o_b, gb, w_out, norm_g, ln_g, ln_b)
    wb = k_past.shape[1]
    return y, k_ext[:, T:T + wb], v_ext[:, T:T + wb], S.astype(S0.dtype)

def setup_inputs(seed: int = 0) -> dict:
    key = jax.random.key(seed)
    ks = jax.random.split(key, 12)
    win_buf = min(WINDOW_MAX, PAST_LEN)
    x_prompt = jax.random.normal(ks[0], (BATCH, SEQ, D_MODEL), jnp.float32)
    x_sample = jax.random.normal(ks[1], (DEC_BATCH, DEC_SEQ, D_MODEL), jnp.float32)
    cache_k = jax.random.normal(ks[2], (DEPTH, DEC_BATCH, win_buf, N_HEADS_A, HEAD_DIM_A), jnp.float32)
    cache_v = jax.random.normal(ks[3], (DEPTH, DEC_BATCH, win_buf, N_HEADS_A, HEAD_DIM_A), jnp.float32) * BETA
    state_hgrn = jax.random.normal(ks[4], (DEPTH, DEC_BATCH, N_HEADS_B, EXPAND_B, HEAD_V_B), jnp.float32) * 0.5
    col_scale = jnp.ones((D_IN,), jnp.float32)
    col_scale = col_scale.at[2 * D_A:3 * D_A].set(BETA)
    col_scale = col_scale.at[4 * D_A + 2 * D_F:4 * D_A + 2 * D_F + D_B].set(BETA)
    w_in = jax.random.normal(ks[5], (DEPTH, D_MODEL, D_IN), jnp.float32) * (D_MODEL ** -0.5) * col_scale
    w_out = jax.random.normal(ks[6], (DEPTH, D_MIX, D_MODEL), jnp.float32) * (D_MIX ** -0.5) * BETA
    rel_bias = jax.random.normal(ks[7], (NUM_BUCKETS, N_HEADS_A), jnp.float32) * 0.5
    lb_param = jax.random.normal(ks[8], (DEPTH + 1, D_F), jnp.float32) * 0.5
    hgrn_norm_g = 1.0 + 0.05 * jax.random.normal(ks[9], (DEPTH, HEAD_V_B), jnp.float32)
    ln_g = 1.0 + 0.05 * jax.random.normal(ks[10], (DEPTH, D_MODEL), jnp.float32)
    ln_b = 0.02 * jax.random.normal(ks[11], (DEPTH, D_MODEL), jnp.float32)
    return {"x_prompt": x_prompt, "x_sample": x_sample, "cache_k": cache_k, "cache_v": cache_v,
            "state_hgrn": state_hgrn, "w_in": w_in, "w_out": w_out, "rel_bias": rel_bias,
            "lb_param": lb_param, "hgrn_norm_g": hgrn_norm_g, "ln_g": ln_g, "ln_b": ln_b}

def reference(x_prompt, x_sample, cache_k, cache_v, state_hgrn, w_in, w_out, rel_bias,
              lb_param, hgrn_norm_g, ln_g, ln_b):
    lb_all = jnp.cumsum(jax.nn.softmax(lb_param.astype(jnp.float32), axis=0), axis=0)
    yp, ys = x_prompt, x_sample
    kp_l, vp_l, sp_l, ks_l, vs_l, ss_l = [], [], [], [], [], []
    for l in range(DEPTH):
        yp, kp, vp, sp = _prompt_layer(yp, w_in[l], w_out[l], rel_bias, lb_all[l],
                                       hgrn_norm_g[l], ln_g[l], ln_b[l])
        ys, k_s, v_s, s_s = _sample_layer(ys, cache_k[l], cache_v[l], state_hgrn[l], w_in[l], w_out[l],
                                          rel_bias, lb_all[l], hgrn_norm_g[l], ln_g[l], ln_b[l])
        kp_l.append(kp)
        vp_l.append(vp)
        sp_l.append(sp)
        ks_l.append(k_s)
        vs_l.append(v_s)
        ss_l.append(s_s)
    return (yp, ys, jnp.stack(kp_l), jnp.stack(vp_l), jnp.stack(ks_l), jnp.stack(vs_l),
            jnp.stack(sp_l), jnp.stack(ss_l))


_drawn_inputs = setup_inputs


def setup_inputs(seed=0):
    import zlib

    import numpy as np

    out = dict(_drawn_inputs(seed))
    spreads = {}
    factors = {'rel_bias': 8.0, 'hgrn_norm_g': 4.879, 'ln_b': 2.835}
    for name, (base, spread) in spreads.items():
        noise = np.random.default_rng([zlib.crc32(name.encode()), seed]).standard_normal(out[name].shape)
        drawn = base * np.exp(spread * noise) if base else spread * noise
        out[name] = __import__('jax').numpy.asarray(drawn.astype(out[name].dtype))
    for name, factor in factors.items():
        out[name] = (out[name] * factor).astype(out[name].dtype)
    return out
```

```python
from contextlib import ExitStack

import numpy as np
import concourse.bass as bass
from concourse import mybir

F32 = mybir.dt.float32
F32R = mybir.dt.float32r
I32 = mybir.dt.int32
ALU = mybir.AluOpType
ACT = mybir.ActivationFunctionType
AX = mybir.AxisListType.X

P = 128
D = 1024
KD = D // P
T = 2048
NB, NT = 8, 8
TS = NB * NT
TT = T + TS
HA, DA = 8, 64
WA = HA * DA
NG = HA // 2
HB, DB = 4, 128
WB = HB * DB
WIN = 2048
DILS = (1, 4, 16)
NC = len(DILS)
BAND = 128
BUCKETS, MAX_DIST = 32, 2048
SCALE = DA ** -0.5
ALPHA = 2.0 ** 0.25
EPS = 1e-5
NEG = -1e30

NCT = 16
WN = 2048
OW = DA + 2
CH = 64
SEG = 512
NSEG = T // SEG
NPR = SEG // P
LEVELS = (32, 16, 8, 4, 2, 1)
LB = 3 * BAND
LD = WIN + 2 * NT


def shape_constants():
    def buckets(dist):
        exact = BUCKETS // 2
        d = np.maximum(dist, 1).astype(np.float32)
        large = exact + (np.log(d / exact) / np.log(MAX_DIST / exact) * (BUCKETS - exact)).astype(np.int32)
        return np.where(dist < exact, dist, np.minimum(large, BUCKETS - 1)).astype(np.int32)

    expand = np.zeros((BUCKETS + 1, NC * LB + LD), np.float32)
    for c, dil in enumerate(DILS):
        for x in range(LB):
            sub = 2 * BAND - 1 - x
            if 0 <= sub <= BAND:
                expand[buckets(np.array([dil * sub]))[0], c * LB + x] = 1 / SCALE
            else:
                expand[BUCKETS, c * LB + x] = NEG
    for x in range(LD):
        dist = WIN + NT - 1 - x
        n = sum(dist >= 0 and dist % dil == 0 and dist // dil <= BAND for dil in DILS)
        if n:
            expand[buckets(np.array([dist]))[0], NC * LB + x] = 1 / SCALE
            expand[BUCKETS, NC * LB + x] = np.log(n) / SCALE
        else:
            expand[BUCKETS, NC * LB + x] = NEG

    def level(h, s, t):
        return (s // (2 * h) == t // (2 * h)) & (s % (2 * h) < h) & (t % (2 * h) >= h)

    def go_on(n, c):
        return np.tile((np.arange(n) % c != 0).astype(np.float32), (P, 1))

    s_of = np.arange(P)[:, None] % CH
    lmask = np.stack([level(h, s_of, (np.arange(CH // 2) // h * 2 * h + h + np.arange(CH // 2) % h)[None])
                      for h in LEVELS], 1)
    ss, st = np.arange(TS)[:, None], np.arange(TS)[None]
    smask = np.stack([level(h, ss, st) for h in LEVELS if h < NT] + [ss == st], 1)
    return {
        "expand": expand, "ident": np.eye(P, dtype=np.float32),
        "go_on": go_on(HB * SEG, CH), "go_on_s": go_on(HB * TS, NT),
        "lmask": lmask.astype(np.int32), "dmask": (s_of == np.arange(CH)[None]).astype(np.int32),
        "smask": smask.astype(np.int32),
        "rowm": (np.arange(TS)[:, None] // NT == np.arange(NB)[None]).astype(np.float32),
    }


def region(ctx, nc):
    def sb(name, shape, dt=F32):
        return ctx.enter_context(nc.sbuf_tensor(name, shape, dt))

    def ps(name, shape):
        return ctx.enter_context(nc.psum_tensor(name, shape, F32))

    def sem(name):
        return ctx.enter_context(nc.semaphore(name))
    return sb, ps, sem


def project_transposed(nc, xT, w_t, projT, cache_kT, cache_v, kwin_s, vwin_s):
    chunks = [(j * 512, min(512, TT - j * 512)) for j in range((TT + 511) // 512)]
    NCH = len(chunks)
    with ExitStack() as ctx:
        sb, ps, sem = region(ctx, nc)
        xhi, xlo = sb("xhi", [P, KD, TT], F32R), sb("xlo", [P, KD, TT], F32R)
        xraw = sb("xraw", [P, 2, KD * 512])
        wraw = sb("wraw", [P, 2, KD, P])
        whi, wlo = sb("whi", [P, 2, KD, P], F32R), sb("wlo", [P, 2, KD, P], F32R)
        stage = sb("stage", [P, 2, TT])
        acc = ps("acc", [P, NCH, 512])
        w_landed = [sem(f"w_landed{u}") for u in range(2)]
        x_landed = [sem(f"x_landed{u}") for u in range(2)]
        stage_free = [sem(f"stage_free{u}") for u in range(2)]
        w_hi, w_split = sem("w_hi"), sem("w_split")
        x_hi, x_split = sem("x_hi"), sem("x_split")
        chunk_done, bank_free, copied = sem("chunk_done"), sem("bank_free"), sem("copied")

        def xraw_of(j):
            n = chunks[j][1]
            return xraw[:, j % 2, 0:KD * n].rearrange("p (k n) -> p k n", k=KD)

        with nc.Block() as block:
            @block.sync
            def _(sp):
                for u in range(2):
                    sp.sem_inc(stage_free[u], 16)
                    sp.dma_start(wraw[:, u], w_t[u]).then_inc(w_landed[u], 16)
                for j, (c0, n) in enumerate(chunks):
                    if j >= 2:
                        sp.wait_ge(x_split, j - 1)
                    sp.dma_start(xraw_of(j), xT[:, :, c0:c0 + n]).then_inc(x_landed[j % 2], 16)

                def store(ct, u):
                    sp.wait_ge(bank_free, NCH * (ct + 2))
                    sp.dma_start(projT[ct], stage[:, u, :]).then_inc(stage_free[u], 16)

                with sp.Fori(0, NCT // 2 - 1) as i:
                    for u in range(2):
                        sp.wait_ge(w_split, 2 * i + u + 1)
                        sp.dma_start(wraw[:, u], w_t[2 * i + 2 + u]).then_inc(w_landed[u], 16)
                        store(2 * i + u, u)
                for u in range(2):
                    store(NCT - 2 + u, u)
                for u in range(2):
                    sp.wait_ge(stage_free[u], 16 * (NCT // 2 + 1))

            @block.gpsimd
            def _(pool):
                for b in range(NB):
                    pool.wait_ge(chunk_done, 1 + 4 * b)
                    pool.dma_start(kwin_s[b, :, 0:WIN - NT], cache_kT[b, :, NT:WIN]).then_inc(copied, 16)
                    pool.dma_start(vwin_s[b, 0:WIN - NT, :], cache_v[b, NT:WIN, :]).then_inc(copied, 16)
                pool.wait_ge(copied, 2 * NB * 16)

            @block.vector
            def _(dve):
                def split_w(ct, u, i):
                    dve.wait_ge(w_landed[u], 16 * (i + 1))
                    nc.vector.tensor_copy(whi[:, u], wraw[:, u]).then_inc(w_hi, 1)
                    dve.wait_ge(w_hi, ct + 1)
                    nc.vector.tensor_tensor(wlo[:, u], wraw[:, u], whi[:, u].bitcast(F32),
                                            ALU.subtract).then_inc(w_split, 1)

                split_w(0, 0, 0)
                for j, (c0, n) in enumerate(chunks):
                    dve.wait_ge(x_hi, j + 1)
                    nc.vector.tensor_tensor(xlo[:, :, c0:c0 + n], xraw_of(j), xhi[:, :, c0:c0 + n].bitcast(F32),
                                            ALU.subtract).then_inc(x_split, 1)
                    if j == 0:
                        split_w(1, 1, 0)
                with dve.Fori(1, NCT // 2) as i:
                    for u in range(2):
                        dve.wait_ge(chunk_done, NCH * (2 * i + u - 1))
                        split_w(2 * i + u, u, i)

            @block.tensor
            def _(pe):
                with pe.Fori(0, NCT // 2) as i:
                    for u in range(2):
                        ct = 2 * i + u
                        pe.wait_ge(w_split, ct + 1)
                        for j, (c0, n) in enumerate(chunks):
                            pe.wait_ge(x_split, j + 1)
                            pe.wait_ge(bank_free, NCH * ct + j + 1)
                            for k in range(KD):
                                for a, (w, x) in enumerate(((whi, xhi), (whi, xlo), (wlo, xhi))):
                                    mm = pe.matmul(acc[:, j, 0:n], w[:, u, k], x[:, k, c0:c0 + n],
                                                   start=(k == 0 and a == 0), stop=(k == KD - 1 and a == 2))
                            mm.then_inc(chunk_done, 1)

            @block.scalar
            def _(act):
                act.sem_inc(bank_free, NCH)
                for j, (c0, n) in enumerate(chunks):
                    act.wait_ge(x_landed[j % 2], 16 * (j // 2 + 1))
                    nc.scalar.activation(xhi[:, :, c0:c0 + n], xraw_of(j), ACT.Copy).then_inc(x_hi, 1)
                for first, last, func in ((0, 4, ACT.Copy), (4, 6, ACT.Silu), (6, 8, ACT.Sigmoid)):
                    with act.Fori(first, last) as i:
                        for u in range(2):
                            act.wait_ge(stage_free[u], 16 * (i + 1))
                            for j, (c0, n) in enumerate(chunks):
                                act.wait_ge(chunk_done, NCH * (2 * i + u) + j + 1)
                                nc.scalar.activation(stage[:, u, c0:c0 + n], acc[:, j, 0:n],
                                                     func).then_inc(bank_free, 1)


def project_natural(nc, xT, w_n, projT, projN, kwin_p, vwin_p, kwin_s, vwin_s):
    NP = T // P // 2
    with ExitStack() as ctx:
        sb, ps, sem = region(ctx, nc)
        whi, wlo = sb("nwhi", [P, KD, WN], F32R), sb("nwlo", [P, KD, WN], F32R)
        wraw = sb("nwraw", [P, 2, WN])
        xraw = sb("nxraw", [P, 2, KD, P])
        xhi, xlo = sb("nxhi", [P, 2, KD, P], F32R), sb("nxlo", [P, 2, KD, P], F32R)
        stage = sb("nstage", [P, 2, WN])
        acc = ps("nacc", [P, 2, 4, 512])
        w_landed = [sem(f"nw_landed{u}") for u in range(2)]
        x_landed = [sem(f"nx_landed{u}") for u in range(2)]
        stage_free = [sem(f"nstage_free{u}") for u in range(2)]
        w_hi, w_split, x_hi, x_split = sem("nw_hi"), sem("nw_split"), sem("nx_hi"), sem("nx_split")
        tile_done, act_out, dve_out = sem("tile_done"), sem("act_out"), sem("dve_out")
        moved, v_out = sem("moved"), sem("v_out")

        with nc.Block() as block:
            @block.sync
            def _(sp):
                def load_x(t, u, n=P):
                    sp.dma_start(xraw[:, u, :, 0:n], xT[:, :, t:t + n] if isinstance(t, int) else
                                 xT[:, :, bass.ds(t, n)]).then_inc(x_landed[u], 16)

                def store(i, u, n=P):
                    sp.wait_ge(act_out, 2 * (2 * i + u) + 4 + 2)
                    sp.wait_ge(dve_out, 2 * (2 * i + u) + 4 + 2)
                    sp.dma_start(projN[bass.ds((2 * i + u) * P, n), :], stage[0:n, u, :]).then_inc(stage_free[u], 16)

                load_x(0, 0)
                for k in range(KD):
                    if k >= 2:
                        sp.wait_ge(w_split, k - 1)
                    sp.dma_start(wraw[:, k % 2], w_n[:, k, :]).then_inc(w_landed[k % 2], 16)
                    if k == 1:
                        load_x(P, 1)
                for u in range(2):
                    sp.sem_inc(stage_free[u], 16)
                with sp.Fori(0, NP - 1) as i:
                    for u in range(2):
                        sp.wait_ge(x_split, 2 * i + u + 1)
                        load_x((2 * i + 2 + u) * P, u)
                        store(i, u)
                sp.wait_ge(x_split, 2 * NP - 1)
                load_x(T, 0, TS)
                store(NP - 1, 0)
                store(NP - 1, 1)
                store(NP, 0, TS)
                for u in range(2):
                    sp.wait_ge(stage_free[u], 16 * (NP + 2 - u))

            @block.gpsimd
            def _(pool):
                for c in range(NG):
                    pool.dma_start(kwin_p[c], projT[NG + c, :, 0:T]).then_inc(moved, 16)
                    for b in range(NB):
                        pool.dma_start(kwin_s[b, c * P:(c + 1) * P, WIN - NT:WIN],
                                       projT[NG + c, :, T + b * NT:T + (b + 1) * NT]).then_inc(moved, 16)
                pool.wait_ge(moved, 16 * NG * (NB + 1))
                pool.wait_ge(stage_free[1], 16 * (NP + 1))
                pool.wait_ge(stage_free[0], 16 * (NP + 2))
                pool.dma_start(vwin_p, projN[0:T, 0:WA]).then_inc(v_out, 16)
                for b in range(NB):
                    pool.dma_start(vwin_s[b, WIN - NT:WIN, :],
                                   projN[T + b * NT:T + (b + 1) * NT, 0:WA]).then_inc(v_out, 16)
                pool.wait_ge(v_out, 16 * (NB + 1))

            @block.vector
            def _(dve):
                def split_x(t, i, u, n=P):
                    dve.wait_ge(x_landed[u], 16 * (i + 1))
                    nc.vector.tensor_copy(xhi[:, u, :, 0:n], xraw[:, u, :, 0:n]).then_inc(x_hi, 1)
                    dve.wait_ge(x_hi, t + 1)
                    nc.vector.tensor_tensor(xlo[:, u, :, 0:n], xraw[:, u, :, 0:n], xhi[:, u, :, 0:n].bitcast(F32),
                                            ALU.subtract).then_inc(x_split, 1)

                def evacuate(t, i, u, n=P):
                    dve.wait_ge(tile_done, t + 1)
                    dve.wait_ge(stage_free[u], 16 * (i + 1))
                    for g in (0, 2):
                        nc.vector.tensor_copy(stage[0:n, u, g * 512:(g + 1) * 512],
                                              acc[0:n, u, g, :]).then_inc(dve_out, 1)

                dve.sem_inc(dve_out, 4)
                split_x(0, 0, 0)
                for k in range(KD):
                    dve.wait_ge(w_landed[k % 2], 16 * (k // 2 + 1))
                    dve.wait_ge(w_hi, k + 1)
                    nc.vector.tensor_tensor(wlo[:, k], wraw[:, k % 2], whi[:, k].bitcast(F32),
                                            ALU.subtract).then_inc(w_split, 1)
                split_x(1, 0, 1)
                with dve.Fori(0, NP - 1) as i:
                    for u in range(2):
                        dve.wait_ge(tile_done, 2 * i + u + 1)
                        split_x(2 * i + 2 + u, i + 1, u)
                        evacuate(2 * i + u, i, u)
                dve.wait_ge(tile_done, 2 * NP - 1)
                split_x(2 * NP, NP, 0, TS)
                evacuate(2 * NP - 2, NP - 1, 0)
                evacuate(2 * NP - 1, NP - 1, 1)
                evacuate(2 * NP, NP, 0, TS)

            @block.tensor
            def _(pe):
                def tile(t, u, n=P, first=False):
                    pe.wait_ge(x_split, t + 1)
                    pe.wait_ge(dve_out, 2 * t + 2)
                    pe.wait_ge(act_out, 2 * t + 2)
                    for k in range(KD):
                        if first:
                            pe.wait_ge(w_split, k + 1)
                        for a, (x, w) in enumerate(((xhi, whi), (xhi, wlo), (xlo, whi))):
                            for g in range(4):
                                mm = pe.matmul(acc[0:n, u, g, :], x[:, u, k, 0:n], w[:, k, g * 512:(g + 1) * 512],
                                               start=(k == 0 and a == 0), stop=(k == KD - 1 and a == 2))
                    mm.then_inc(tile_done, 1)

                tile(0, 0, first=True)
                tile(1, 1)
                with pe.Fori(1, NP) as i:
                    for u in range(2):
                        tile(2 * i + u, u)
                tile(2 * NP, 0, TS)

            @block.scalar
            def _(act):
                act.sem_inc(act_out, 4)
                for k in range(KD):
                    act.wait_ge(w_landed[k % 2], 16 * (k // 2 + 1))
                    nc.scalar.activation(whi[:, k], wraw[:, k % 2], ACT.Copy).then_inc(w_hi, 1)

                def evacuate(t, i, u, n=P):
                    act.wait_ge(tile_done, t + 1)
                    act.wait_ge(stage_free[u], 16 * (i + 1))
                    for g in (1, 3):
                        nc.scalar.activation(stage[0:n, u, g * 512:(g + 1) * 512], acc[0:n, u, g, :],
                                             ACT.Silu).then_inc(act_out, 1)
                with act.Fori(0, NP) as i:
                    for u in range(2):
                        evacuate(2 * i + u, i, u)
                evacuate(2 * NP, NP, 0, TS)




def bias_vectors(nc, rel_bias, expand, rep_p, rep_d):
    N = NC * LB + LD
    parts = [(x, min(512, N - x)) for x in range(0, N, 512)]
    with ExitStack() as ctx:
        sb, ps, sem = region(ctx, nc)
        table = sb("table", [BUCKETS + 1, HA])
        exp_sb = sb("expand_sb", [BUCKETS + 1, N])
        vec = sb("vec", [HA, N])
        acc = ps("vec_acc", [HA, len(parts), 512])
        one_set, landed, product, copied, kept, repeated = (
            sem(n) for n in ("bv_one", "bv_landed", "bv_product", "bv_copied", "bv_kept", "bv_repeated"))
        vec_dram = nc.dram_tensor("bias_vec", [HA, N], F32, kind="Internal").ap()
        with nc.Block() as block:
            @block.vector
            def _(dve):
                nc.vector.memset(table[:], 1.0).then_inc(one_set, 1)
                for n, (x, w) in enumerate(parts):
                    dve.wait_ge(product, n + 1)
                    nc.vector.tensor_copy(vec[:, x:x + w], acc[:, n, 0:w]).then_inc(copied, 1)

            @block.tensor
            def _(pe):
                pe.wait_ge(landed, 32)
                for n, (x, w) in enumerate(parts):
                    pe.matmul(acc[:, n, 0:w], table[:], exp_sb[:, x:x + w], start=True, stop=True).then_inc(product, 1)

            @block.sync
            def _(sp):
                sp.dma_start(exp_sb[:], expand).then_inc(landed, 16)
                sp.wait_ge(one_set, 1)
                sp.dma_start(table[0:BUCKETS, :], rel_bias).then_inc(landed, 16)
                sp.wait_ge(copied, len(parts))
                sp.dma_start(vec_dram, vec[:]).then_inc(kept, 16)
                sp.wait_ge(kept, 16)
                L = NC * LB
                sp.dma_start(rep_p, bass.AP(tensor=vec_dram.tensor, offset=0, ap=[[0, P], [N, HA], [1, L]])
                             ).then_inc(repeated, 16)
                sp.dma_start(rep_d, bass.AP(tensor=vec_dram.tensor, offset=L, ap=[[0, NT], [N, HA], [1, LD]])
                             ).then_inc(repeated, 16)
                sp.wait_ge(repeated, 32)


def hgrn_prompt(nc, projT, projN, lbT, scan_mask, level_masks, diag_mask, ident_d, o_b, state_out):
    NS = HB * SEG
    with ExitStack() as ctx:
        sb, ps, sem = region(ctx, nc)
        lbp = sb("lbp", [P, 2, HB])
        lbm, lb, oml, noml = (sb(n, [P, HB]) for n in ("lbm", "lb", "oml", "noml"))
        reset = sb("reset", [P, NS])
        lmask = sb("lmask", [P, len(LEVELS), CH // 2], I32)
        dmask = sb("dmask", [P, CH], I32)
        ident = sb("ident3", [P, P])
        q, sg = sb("q", [P, 2, HB, SEG]), sb("sg", [P, 2, HB, SEG])
        v = sb("v3", [P, 2, NPR, WB])
        k, g, b, eb, qe, kh = (sb(n, [P, HB, SEG]) for n in ("k3", "g3", "b3", "eb", "qe", "kh"))
        diff, ed = sb("diff", [P, 2, NS]), sb("ed", [P, 2, NS])
        kl, ql = sb("kl", [P, 2, HB, SEG]), sb("ql", [P, 2, HB, SEG // 2])
        at = sb("at", [P, NPR, HB, CH])
        khn = sb("khn", [P, NPR, WB])
        S = sb("S", [P, 2, HB, DB])
        ost = sb("ost", [P, 2, NPR, WB])
        a_ps = ps("a_ps", [P, 2, 512])
        t_ps, o_ps, s_ps = ps("t_ps", [P, 2, 512]), ps("o_ps", [P, 2, 512]), ps("s_ps", [P, 2, 512])
        landed = [sem(f"h_landed{u}") for u in range(2)]
        ost_free = [sem(f"ost_free{u}") for u in range(2)]
        const, state_kept, mask_begun = sem("h_const"), sem("state_kept"), sem("mask_begun")
        lbs, bounds, ready = sem("h_lbs"), sem("h_bounds"), sem("h_ready")
        g_done, k_done, b_done, eb_done, qe_done = (sem(n) for n in ("g_done", "k_done", "b_done", "eb_done", "qe_done"))
        d_done, e_done, prod_done, a_done, mask_done = (sem(n) for n in ("d_done", "e_done", "prod_done", "a_done", "mask_done"))
        chain, t_done, khn_done = sem("chain"), sem("t_done"), sem("khn_done")
        ds_done, s_done, o_done, o_out = sem("ds_done"), sem("s_done"), sem("o_done"), sem("o_out")
        NL = len(LEVELS)
        ND = NL + 1
        NA = NL + 2
        NCK = 2 * NPR

        with nc.Block() as block:
            @block.sync
            def _(sp):
                for dst, src in ((lbp[:], lbT), (reset[:], scan_mask), (lmask[:], level_masks),
                                 (dmask[:], diag_mask), (ident[:], ident_d)):
                    sp.dma_start(dst, src).then_inc(const, 16)

                def load(s):
                    u, t0 = s % 2, s * SEG
                    sp.dma_start(sg[:, u], projT[12:16, :, t0:t0 + SEG].rearrange("h p t -> p h t")).then_inc(landed[u], 16)
                    sp.dma_start(q[:, u], projT[8:12, :, t0:t0 + SEG].rearrange("h p t -> p h t")).then_inc(landed[u], 16)
                    sp.dma_start(v[:, u], projN[t0:t0 + SEG, 2 * WB:3 * WB].rearrange("(c p) v -> p c v", p=P)
                                 ).then_inc(landed[u], 16)

                def store(s):
                    u, t0 = s % 2, s * SEG
                    sp.wait_ge(o_out, NPR * (s + 1) + 2)
                    sp.dma_start(o_b[t0:t0 + SEG, :].rearrange("(c p) v -> p c v", p=P), ost[:, u]).then_inc(ost_free[u], 16)

                for u in range(2):
                    sp.sem_inc(ost_free[u], 16)
                load(0)
                load(1)
                for s in range(NSEG):
                    store(s)
                    if s + 2 < NSEG:
                        sp.wait_ge(o_done, NPR * (s + 1) + 1)
                        load(s + 2)
                sp.wait_ge(s_done, NSEG * NCK + 1)
                sp.dma_start(state_out.rearrange("h k v -> k h v"), S[:, 0]).then_inc(state_kept, 16)
                sp.wait_ge(state_kept, 16)
                for u in range(2):
                    sp.wait_ge(ost_free[u], 16 * (NSEG // 2 + 1))

            @block.scalar
            def _(act):
                act.wait_ge(lbs, 1)
                nc.scalar.activation(lbp[:], lbp[:], ACT.Exp).then_inc(lbs, 1)
                act.wait_ge(bounds, 1)
                act.sem_inc(khn_done, 2)
                with act.Fori(0, NSEG // 2) as i:
                    for u in range(2):
                        s = 2 * i + u
                        act.wait_ge(landed[u], 48 * (i + 1))
                        act.wait_ge(b_done, s + 1)
                        for h in range(HB):
                            ins = nc.scalar.activation(g[:, h], sg[:, u, h], ACT.Ln, bias=lb[:, h:h + 1], scale=oml[:, h:h + 1])
                        ins.then_inc(g_done, 1)
                        act.wait_ge(b_done, s + 2)
                        act.wait_ge(qe_done, s + 1)
                        act.wait_ge(s_done, NCK * s + 1)
                        nc.scalar.activation(eb[:], b[:], ACT.Exp).then_inc(eb_done, 1)
                        for n in range(ND):
                            act.wait_ge(d_done, ND * s + n + 1)
                            act.wait_ge(prod_done, ND * s + max(n + 1, 2))
                            h2 = LEVELS[n] if n < NL else None
                            if h2:
                                dv = diff[:, n % 2, :].rearrange("p (n two h) -> p n two h", two=2, h=h2)
                                ev = ed[:, n % 2, :].rearrange("p (n two h) -> p n two h", two=2, h=h2)
                                nc.scalar.activation(ev[:, :, 0], dv[:, :, 0], ACT.Exp, scale=-1.0)
                                nc.scalar.activation(ev[:, :, 1], dv[:, :, 1], ACT.Exp).then_inc(e_done, 1)
                            else:
                                nc.scalar.activation(ed[:, n % 2, :], diff[:, n % 2, :], ACT.Exp, scale=-1.0).then_inc(e_done, 1)
                        act.wait_ge(o_done, NPR * s + 1)
                        for c in range(NPR):
                            act.wait_ge(t_done, NPR * s + c + 1)
                            nc.scalar.activation(khn[:, c], t_ps[:, c % 2], ACT.Copy).then_inc(khn_done, 1)
                        act.wait_ge(ost_free[u], 16 * (i + 1))
                        for c in range(NPR):
                            act.wait_ge(o_done, NPR * s + c + 2)
                            nc.scalar.activation(ost[:, u, c], o_ps[:, c % 2], ACT.Copy).then_inc(o_out, 1)

            @block.gpsimd
            def _(pool):
                nc.gpsimd.memset(kl[:], 0.0).then_inc(ready, 1)
                with pool.Fori(0, NSEG) as s:
                    pool.wait_ge(b_done, s + 2)
                    for n in range(ND):
                        pool.wait_ge(e_done, ND * s + max(n + 1, 2))
                        m = LEVELS[n] if n < NL else CH // 2
                        mid = m - 1 if n < NL else CH - 1
                        bv = b[:].rearrange("p h (n w) -> p (h n) w", w=2 * m)
                        dv = diff[:, n % 2, :].rearrange("p (n w) -> p n w", w=2 * m)
                        nc.gpsimd.tensor_tensor(dv, bv, bv[:, :, mid:mid + 1].to_broadcast([P, NS // (2 * m), 2 * m]),
                                                ALU.subtract).then_inc(d_done, 1)

            @block.vector
            def _(dve):
                dve.wait_ge(const, 16 * 5)
                steps = [0]

                def then(ins):
                    steps[0] += 1
                    ins.then_inc(chain, 1)
                    dve.wait_ge(chain, steps[0])

                then(nc.vector.tensor_tensor(lbm[:], lbp[:, 0], lbp[:, 1], ALU.max))
                for r in range(2):
                    ins = nc.vector.tensor_tensor(lbp[:, r], lbp[:, r], lbm[:], ALU.subtract)
                    if r == 0:
                        then(ins)
                ins.then_inc(lbs, 1)
                dve.wait_ge(lbs, 2)
                then(nc.vector.tensor_tensor(lbm[:], lbp[:, 0], lbp[:, 1], ALU.add))
                then(nc.vector.reciprocal(lbm[:], lbm[:]))
                then(nc.vector.tensor_tensor(lb[:], lbp[:, 0], lbm[:], ALU.mult))
                then(nc.vector.tensor_scalar(oml[:], lb[:], -1.0, 1.0, ALU.mult, ALU.add))
                nc.vector.tensor_scalar(noml[:], oml[:], -1.0, None, ALU.mult).then_inc(bounds, 1)
                dve.wait_ge(bounds, 1)
                nc.vector.memset(at[:], 0.0)
                nc.vector.memset(S[:, 0], 0.0).then_inc(s_done, 1)
                dve.wait_ge(s_done, 1)
                dve.wait_ge(ready, 1)
                dve.sem_inc(e_done, 2)
                dve.sem_inc(prod_done, 2)
                dve.sem_inc(mask_done, 2)
                dve.sem_inc(qe_done, 1)
                dve.sem_inc(o_done, 1)
                dve.sem_inc(o_out, 2)
                dve.sem_inc(b_done, 1)

                def mask_step(s, n):
                    dve.wait_ge(mask_done, NA * s + n + 2)
                    dve.wait_ge(a_done, NA * s + n + 1)
                    dve.sem_inc(mask_begun, 1)
                    if n < NL:
                        h2 = LEVELS[n]
                        nb = CH // (2 * h2)
                        dst = at[:].rearrange("p c h (n two j) -> p (c h) n two j", two=2, j=h2)[:, :, :, 1, :]
                        src = a_ps[:, n % 2, :].rearrange("p (a n j) -> p a n j", n=nb, j=h2)
                        m = lmask[:, n, :].rearrange("p (n j) -> p n j", j=h2).unsqueeze(1).to_broadcast(
                            [P, NPR * HB, nb, h2])
                    else:
                        x = n - NL
                        dst = at[:, 2 * x:2 * x + 2].rearrange("p c h t -> p (c h) t")
                        src = a_ps[:, n % 2, :].rearrange("p (a t) -> p a t", t=CH)
                        m = dmask[:].unsqueeze(1).to_broadcast([P, 2 * HB, CH])
                    nc.vector.copy_predicated(dst, m, src).then_inc(mask_done, 1)

                with dve.Fori(0, NSEG // 2) as i:
                    for u in range(2):
                        s = 2 * i + u
                        dve.wait_ge(landed[u], 48 * (i + 1))
                        for h in range(HB):
                            ins = nc.vector.tensor_scalar(k[:, h], sg[:, u, h], noml[:, h:h + 1], oml[:, h:h + 1],
                                                          ALU.mult, ALU.add)
                        ins.then_inc(k_done, 1)
                        dve.wait_ge(g_done, s + 1)
                        nc.vector.tensor_tensor_scan(b[:].rearrange("p h t -> p (h t)"), reset[:],
                                                     g[:].rearrange("p h t -> p (h t)"), 0.0,
                                                     ALU.mult, ALU.add).then_inc(b_done, 1)
                        dve.wait_ge(k_done, s + 1)
                        for n in range(ND):
                            dve.wait_ge(e_done, ND * s + n + 3)
                            e = ed[:, n % 2, :]
                            if n < NL:
                                h2 = LEVELS[n]
                                dve.wait_ge(a_done, NA * s + n - 1) if n >= 2 else dve.wait_ge(o_done, NPR * s + 1)
                                cut = lambda ap: ap.rearrange("p (n two j) -> p n two j", two=2, j=h2)
                                kv = cut(k[:].rearrange("p h t -> p (h t)"))
                                qv = cut(q[:, u].rearrange("p h t -> p (h t)"))
                                klv = cut(kl[:, n % 2].rearrange("p h t -> p (h t)"))
                                qlv = ql[:, n % 2].rearrange("p h t -> p (h t)").rearrange("p (n j) -> p n j", j=h2)
                                nc.vector.tensor_tensor(klv[:, :, 0], kv[:, :, 0], cut(e)[:, :, 0], ALU.mult)
                                nc.vector.tensor_tensor(qlv, qv[:, :, 1], cut(e)[:, :, 1], ALU.mult).then_inc(prod_done, 1)
                                if n:
                                    mask_step(s, n - 1)
                            else:
                                nc.vector.tensor_tensor(kh[:].rearrange("p h t -> p (h t)"), k[:].rearrange("p h t -> p (h t)"),
                                                        e, ALU.mult).then_inc(prod_done, 1)
                        dve.wait_ge(eb_done, s + 1)
                        nc.vector.tensor_tensor(qe[:], q[:, u], eb[:], ALU.mult).then_inc(qe_done, 1)
                        for n in range(NL - 1, NA):
                            mask_step(s, n)
                        for c in range(NCK):
                            dve.wait_ge(ds_done, NCK * s + c + 1)
                            dve.wait_ge(s_done, NCK * s + c + 1)
                            for h in range(HB):
                                ins = nc.vector.scalar_tensor_tensor(
                                    S[:, (c + 1) % 2, h], S[:, c % 2, h], eb[:, h, (c + 1) * CH - 1:(c + 1) * CH],
                                    s_ps[:, c % 2, h * DB:(h + 1) * DB], ALU.mult, ALU.add)
                            ins.then_inc(s_done, 1)

            @block.tensor
            def _(pe):
                with pe.Fori(0, NSEG // 2) as i:
                    for u in range(2):
                        s = 2 * i + u

                        def a_step(n):
                            pe.wait_ge(mask_done, NA * s + n + 1)
                            if n < NL:
                                pe.wait_ge(prod_done, ND * s + n + 3)
                                todo = [(c, x, h) for c in range(NPR) for x in range(2) for h in range(HB)]
                            else:
                                pe.wait_ge(k_done, s + 1)
                                todo = [(c, x, h) for c in (2 * (n - NL), 2 * (n - NL) + 1) for x in range(2) for h in range(HB)]
                            for c, x, h in todo:
                                t0 = (2 * c + x) * CH
                                if n < NL:
                                    lhs, rhs = kl[:, n % 2, h, t0:t0 + CH], ql[:, n % 2, h, t0 // 2:(t0 + CH) // 2]
                                    col, w = (c * HB + h) * CH // 2, CH // 2
                                else:
                                    lhs, rhs = k[:, h, t0:t0 + CH], q[:, u, h, t0:t0 + CH]
                                    col, w = ((c % 2) * HB + h) * CH, CH
                                mm = pe.matmul(a_ps[x * CH:(x + 1) * CH, n % 2, col:col + w], lhs, rhs, start=True, stop=True)
                            mm.then_inc(a_done, 1)

                        pe.wait_ge(landed[u], 48 * (i + 1))
                        for n in range(NA):
                            a_step(n)
                        pe.wait_ge(prod_done, ND * s + ND + 2)
                        for c in range(NPR):
                            pe.wait_ge(khn_done, NPR * s + c + 1)
                            for h in range(HB):
                                mm = pe.transpose(t_ps[:, c % 2, h * P:(h + 1) * P], kh[:, h, c * P:(c + 1) * P], ident[:])
                            mm.then_inc(t_done, 1)
                        pe.wait_ge(qe_done, s + 2)
                        pe.wait_ge(mask_done, NA * s + NA + 2)
                        for c in range(NCK):
                            r = slice((c % 2) * CH, (c % 2 + 1) * CH)
                            pr = c // 2
                            pe.wait_ge(khn_done, NPR * s + pr + 3)
                            pe.wait_ge(s_done, NCK * s + max(c, 1))
                            for h in range(HB):
                                mm = pe.matmul(s_ps[:, c % 2, h * DB:(h + 1) * DB], khn[r, pr, h * DB:(h + 1) * DB],
                                               v[r, u, pr, h * DB:(h + 1) * DB], start=True, stop=True)
                            mm.then_inc(ds_done, 1)
                            pe.wait_ge(s_done, NCK * s + c + 1)
                            if c % 2 == 0:
                                pe.wait_ge(o_out, NPR * s + pr + 1)
                            for h in range(HB):
                                o = o_ps[r, pr % 2, h * DB:(h + 1) * DB]
                                pe.matmul(o, qe[:, h, c * CH:(c + 1) * CH], S[:, c % 2, h], start=True, stop=False)
                                mm = pe.matmul(o, at[r, pr, h], v[r, u, pr, h * DB:(h + 1) * DB], start=False, stop=True)
                            if c % 2:
                                mm.then_inc(o_done, 1)


def hgrn_sample(nc, projT, projN, lbT, scan_mask, level_masks, row_mask, ident_d, state_in, o_b, state_out):
    N = HB * TS
    levels = [h for h in LEVELS if h < NT]
    NL = len(levels)
    flat = lambda ap: ap.rearrange("p h t -> p (h t)")
    with ExitStack() as ctx:
        sb, ps, sem = region(ctx, nc)
        lbp, lbs_ = sb("s_lbp", [P, 2, HB]), sb("s_lbs", [P, 4, HB])
        reset, masks = sb("s_reset", [P, N]), sb("s_masks", [TS, NL + 1, TS], I32)
        rowm, ident = sb("s_rowm", [TS, NB]), sb("s_ident", [P, P])
        q, sg, v = sb("s_q", [P, HB, TS]), sb("s_sg", [P, HB, TS]), sb("s_v", [TS, WB])
        S0 = sb("s_S0", [P, NB, HB, DB])
        k, g, b, eb, qe, kh, diff, ed = (sb(f"s_{n}", [P, HB, TS]) for n in ("k", "g", "b", "eb", "qe", "kh", "diff", "ed"))
        kl, ql = sb("s_kl", [P, HB, TS]), sb("s_ql", [P, HB, TS])
        at, khn, khm = sb("s_at", [TS, HB, TS]), sb("s_khn", [TS, WB]), sb("s_khm", [TS, NB, WB])
        qem, ost = sb("s_qem", [P, NB, HB, TS]), sb("s_ost", [TS, WB])
        a_ps, t_ps, o_ps, s_ps = ps("s_a_ps", [TS, HB, TS]), ps("s_t_ps", [TS, WB]), ps("s_o_ps", [TS, WB]), ps("s_s_ps", [P, 2, WB])
        landed, stored, chain, act_done, a_done, took = (sem(f"s_{n}") for n in ("landed", "stored", "chain", "act_done", "a_done", "took"))
        t_done, khm_done, ds_done, s_done, o_done, mems = (sem(f"s_{n}") for n in ("t_done", "khm_done", "ds_done", "s_done", "o_done", "mems"))
        lvl = sem("s_lvl")
        with nc.Block() as block:
            @block.sync
            def _(sp):
                for dst, src in ((lbp[:], lbT), (reset[:], scan_mask), (masks[:], level_masks), (rowm[:], row_mask),
                                 (ident[:], ident_d), (q[:], projT[8:12, :, T:TT].rearrange("h p t -> p h t")),
                                 (sg[:], projT[12:16, :, T:TT].rearrange("h p t -> p h t")),
                                 (v[:], projN[T:TT, 2 * WB:3 * WB]),
                                 (S0[:], state_in.rearrange("b h k v -> k b h v"))):
                    sp.dma_start(dst, src).then_inc(landed, 16)
                sp.wait_ge(s_done, NB)
                sp.dma_start(state_out.rearrange("b h k v -> k b h v"), S0[:]).then_inc(stored, 16)
                sp.wait_ge(took, 4 + 1)
                sp.dma_start(o_b[T:TT, :], ost[:]).then_inc(stored, 16)
                sp.wait_ge(stored, 32)

            @block.gpsimd
            def _(pool):
                nc.gpsimd.memset(qem[:], 0.0).then_inc(mems, 1)
                nc.gpsimd.memset(at[:], 0.0).then_inc(mems, 1)

            @block.scalar
            def _(act):
                act.wait_ge(lvl, 1)
                nc.scalar.activation(lbp[:], lbp[:], ACT.Exp).then_inc(act_done, 1)
                act.wait_ge(lvl, 2)
                for h in range(HB):
                    ins = nc.scalar.activation(g[:, h], sg[:, h], ACT.Ln, bias=lbs_[:, 1, h:h + 1], scale=lbs_[:, 2, h:h + 1])
                ins.then_inc(act_done, 1)
                act.wait_ge(lvl, 3)
                nc.scalar.activation(eb[:], b[:], ACT.Exp).then_inc(act_done, 1)
                for n in range(NL + 1):
                    act.wait_ge(lvl, 4 + n)
                    if n < NL:
                        cut = lambda ap: flat(ap).rearrange("p (n two j) -> p n two j", two=2, j=levels[n])
                        nc.scalar.activation(cut(ed[:])[:, :, 0], cut(diff[:])[:, :, 0], ACT.Exp, scale=-1.0)
                        nc.scalar.activation(cut(ed[:])[:, :, 1], cut(diff[:])[:, :, 1], ACT.Exp).then_inc(act_done, 1)
                    else:
                        nc.scalar.activation(ed[:], diff[:], ACT.Exp, scale=-1.0).then_inc(act_done, 1)

            @block.vector
            def _(dve):
                steps = [0]

                def then(ins, more=None):
                    steps[0] += 1
                    ins.then_inc(chain, 1)
                    dve.wait_ge(chain, steps[0])
                    if more is not None:
                        dve.sem_inc(more, 1)

                tt = nc.vector.tensor_tensor
                dve.wait_ge(landed, 16 * 9)
                then(tt(lbs_[:, 0], lbp[:, 0], lbp[:, 1], ALU.max))
                then(tt(lbp[:, 0], lbp[:, 0], lbs_[:, 0], ALU.subtract))
                then(tt(lbp[:, 1], lbp[:, 1], lbs_[:, 0], ALU.subtract), lvl)
                dve.wait_ge(act_done, 1)
                then(tt(lbs_[:, 0], lbp[:, 0], lbp[:, 1], ALU.add))
                then(nc.vector.reciprocal(lbs_[:, 0], lbs_[:, 0]))
                then(tt(lbs_[:, 1], lbp[:, 0], lbs_[:, 0], ALU.mult))
                then(nc.vector.tensor_scalar(lbs_[:, 2], lbs_[:, 1], -1.0, 1.0, ALU.mult, ALU.add))
                then(nc.vector.tensor_scalar(lbs_[:, 3], lbs_[:, 2], -1.0, None, ALU.mult), lvl)
                for h in range(HB):
                    then(nc.vector.tensor_scalar(k[:, h], sg[:, h], lbs_[:, 3, h:h + 1], lbs_[:, 2, h:h + 1], ALU.mult, ALU.add))
                dve.wait_ge(act_done, 2)
                then(nc.vector.tensor_tensor_scan(flat(b[:]), reset[:], flat(g[:]), 0.0, ALU.mult, ALU.add), lvl)
                dve.wait_ge(mems, 2)
                for n in range(NL + 1):
                    w, mid = (2 * levels[n], levels[n] - 1) if n < NL else (NT, NT - 1)
                    bv = flat(b[:]).rearrange("p (n w) -> p n w", w=w)
                    then(tt(flat(diff[:]).rearrange("p (n w) -> p n w", w=w), bv,
                            bv[:, :, mid:mid + 1].to_broadcast([P, N // w, w]), ALU.subtract), lvl)
                    dve.wait_ge(act_done, 4 + n)
                    if n == NL:
                        break
                    then(tt(kl[:], k[:], ed[:], ALU.mult))
                    then(tt(ql[:], q[:], ed[:], ALU.mult), took)
                    dve.wait_ge(a_done, n + 1)
                    then(nc.vector.copy_predicated(at[:], masks[:, n].unsqueeze(1).to_broadcast([TS, HB, TS]), a_ps[:]))
                then(tt(kh[:], k[:], ed[:], ALU.mult), took)
                dve.wait_ge(a_done, NL + 1)
                then(nc.vector.copy_predicated(at[:], masks[:, NL].unsqueeze(1).to_broadcast([TS, HB, TS]), a_ps[:]))
                then(tt(qe[:], q[:], eb[:], ALU.mult))
                for s in range(NB):
                    c = slice(s * NT, (s + 1) * NT)
                    ins = nc.vector.tensor_copy(qem[:, s, :, c], qe[:, :, c])
                ins.then_inc(khm_done, 1)
                dve.wait_ge(t_done, 1)
                then(nc.vector.tensor_copy(khn[:], t_ps[:]))
                for s in range(NB):
                    ins = nc.vector.tensor_scalar(khm[:, s], khn[:], rowm[:, s:s + 1], None, ALU.mult)
                ins.then_inc(khm_done, 1)
                dve.wait_ge(o_done, 1)
                then(nc.vector.tensor_copy(ost[:], o_ps[:]), took)
                for s in range(NB):
                    dve.wait_ge(ds_done, s + 1)
                    for h in range(HB):
                        e = s * NT + NT - 1
                        ins = nc.vector.scalar_tensor_tensor(S0[:, s, h], S0[:, s, h], eb[:, h, e:e + 1],
                                                             s_ps[:, s % 2, h * DB:(h + 1) * DB], ALU.mult, ALU.add)
                    ins.then_inc(s_done, 1)

            @block.tensor
            def _(pe):
                for n in range(NL + 1):
                    pe.wait_ge(took, n + 1)
                    lhs, rhs = (kl, ql) if n < NL else (k, q)
                    for h in range(HB):
                        mm = pe.matmul(a_ps[:, h], lhs[:, h], rhs[:, h], start=True, stop=True)
                    mm.then_inc(a_done, 1)
                for h in range(HB):
                    mm = pe.transpose(t_ps[:, h * P:(h + 1) * P], kh[:, h], ident[:])
                mm.then_inc(t_done, 1)
                pe.wait_ge(khm_done, 1)
                for h in range(HB):
                    o = o_ps[:, h * DB:(h + 1) * DB]
                    for s in range(NB):
                        pe.matmul(o, qem[:, s, h], S0[:, s, h], start=(s == 0), stop=False)
                    mm = pe.matmul(o, at[:, h], v[:, h * DB:(h + 1) * DB], start=False, stop=True)
                mm.then_inc(o_done, 1)
                pe.wait_ge(khm_done, 2)
                for s in range(NB):
                    if s >= 2:
                        pe.wait_ge(s_done, s - 1)
                    for h in range(HB):
                        mm = pe.matmul(s_ps[:, s % 2, h * DB:(h + 1) * DB], khm[:, s, h * DB:(h + 1) * DB],
                                       v[:, h * DB:(h + 1) * DB], start=True, stop=True)
                    mm.then_inc(ds_done, 1)


def attention_prompt(nc, projT, projN, rep_p, ident_d, partials):
    NBK = T // P
    units = []
    for c in range(NC):
        for x in range(2):
            for b in range(0, NBK, 2):
                units.append((c, x, b))
    NU = len(units)
    NGRP = NU // 4

    def block_keys(c, b):
        d = DILS[c]
        nj = NBK // d
        r, j = b // nj, b % nj
        q0 = r + d * P * j
        return (q0, q0 - d * P, 2) if j else (q0, q0, 1)

    def tiles(c, b0):
        out = []
        for y in range(2):
            n = block_keys(c, b0 + y)[2]
            out += [(y, b0 + y - n + 1 + m, 2 - n + m) for m in range(n)]
        return out

    with ExitStack() as ctx:
        sb, ps, sem = region(ctx, nc)
        ident = sb("a_ident", [P, P])
        qT, kT = sb("a_qT", [P, 2, T]), sb("a_kT", [P, 2, T])
        v = sb("a_v", [P, 2, NC, NBK, P])
        bias = sb("a_bias", [P, 2, 2, NC, 2 * P])
        prob = sb("a_prob", [P, 4, 2, 2 * P])
        probT = sb("a_probT", [P, 3, 4, P])
        stage = sb("a_stage", [P, 2, NBK, 2, OW])
        s_ps, t_ps, o_ps = ps("a_s_ps", [P, 3, 512]), ps("a_t_ps", [P, 3, 512]), ps("a_o_ps", [P, 2, 512])
        landed = [sem(f"a_landed{u}") for u in range(2)]
        stage_free = [sem(f"a_stage_free{w}") for w in range(2)]
        const, s_done, p_done, p_turn, e_done = (sem(f"a_{n}") for n in ("const", "s_done", "p_done", "p_turn", "e_done"))
        t_done, pt_done, pv_done, o_out = (sem(f"a_{n}") for n in ("t_done", "pt_done", "pv_done", "o_out"))
        NLD = 10

        with nc.Block() as block:
            @block.sync
            def _(sp):
                sp.dma_start(ident[:], ident_d).then_inc(const, 16)
                sp.sem_inc(stage_free[0], 16)
                sp.sem_inc(stage_free[1], 16)

                def load(g):
                    u = g % 2
                    sp.dma_start(qT[:, u], projT[g, :, 0:T]).then_inc(landed[u], 16)
                    sp.dma_start(kT[:, u], projT[NG + g, :, 0:T]).then_inc(landed[u], 16)
                    L = HA * NC * LB
                    for x in range(2):
                        src = bass.AP(tensor=rep_p.tensor, offset=(2 * g + x) * NC * LB + P - 1,
                                      ap=[[L - 1, P], [LB, NC], [1, 2 * P]])
                        sp.dma_start(bias[:, u, x], src).then_inc(landed[u], 16)
                    for c, d in enumerate(DILS):
                        rows = projN[0:T, g * P:(g + 1) * P].rearrange("(j p r) d -> p r j d", p=P, r=d)
                        dst = v[:, u, c].rearrange("p (r j) d -> p r j d", r=d)
                        if c == 1:
                            for j in range(NBK // d):
                                sp.dma_start(dst[:, :, j], rows[:, :, j]).then_inc(landed[u], 16)
                        else:
                            sp.dma_start(dst[:, 0] if d == 1 else dst[:, :, 0], rows[:, 0] if d == 1 else rows[:, :, 0]
                                         ).then_inc(landed[u], 16)

                load(0)
                load(1)
                for g in range(NG):
                    for c, d in enumerate(DILS):
                        w = (NC * g + c) % 2
                        sp.wait_ge(o_out, NGRP * g + NGRP // NC * (c + 1) + 2)
                        rows = partials[c, :, 2 * g:2 * g + 2, :].rearrange("(j p r) h w -> p r j (h w)", p=P, r=d)
                        src = stage[:, w].rearrange("p (r j) h w -> p r j (h w)", r=d)
                        n = 0
                        if c == 1:
                            for j in range(NBK // d):
                                sp.dma_start(rows[:, :, j], src[:, :, j]).then_inc(stage_free[w], 16)
                        else:
                            a, b = (rows[:, 0], src[:, 0]) if d == 1 else (rows[:, :, 0], src[:, :, 0])
                            for half in range(4):
                                m = NBK // 4
                                sp.dma_start(a[:, half * m:(half + 1) * m], b[:, half * m:(half + 1) * m]
                                             ).then_inc(stage_free[w], 16)
                    if g + 2 < NG:
                        sp.wait_ge(pv_done, NU * (g + 1) + 3)
                        load(g + 2)
                for w in range(2):
                    sp.wait_ge(stage_free[w], 16 + 64 * NC * NG // 2)

            def stage_slot(u, c):
                return (NC * u + c) % 2

            @block.vector
            def _(dve):
                dve.sem_inc(p_done, 3)
                dve.sem_inc(pt_done, 3)
                dve.sem_inc(o_out, 2)
                with dve.Fori(0, NG // 2) as i:
                    for u in range(2):
                        g = 2 * i + u
                        dve.wait_ge(landed[u], 16 * NLD * (i + 1))
                        for n in range(NU + 3):
                            if n < NU:
                                c, x, b = units[n]
                                w = stage_slot(u, c)
                                if n % (NU // NC) == 0:
                                    k = len([1 for m in range(NC * u + c) if m % 2 == w])
                                    dve.wait_ge(stage_free[w], 16 + 64 * (NC * i + k))
                                dve.wait_ge(t_done, NU * g + n + 1)
                                dve.wait_ge(s_done, NU * g + n + 1)
                                dve.sem_inc(p_turn, 1)
                                for y in range(2):
                                    m = P * block_keys(c, b + y)[2]
                                    ins = nc.vector.tensor_tensor_reduce(
                                        prob[:, n % 4, y, 2 * P - m:], s_ps[:, n % 3, y * 2 * P + 2 * P - m:(y + 1) * 2 * P],
                                        bias[:, u, x, c, 2 * P - m:], -SCALE, 3e38, ALU.add, ALU.min,
                                        stage[:, w, b + y, x, DA + 1:DA + 2])
                                ins.then_inc(p_done, 1)
                            if n >= 3:
                                m = n - 3
                                width = P * len(tiles(units[m][0], units[m][2]))
                                dve.wait_ge(pv_done, NU * g + m + 1)
                                dve.wait_ge(t_done, NU * g + m + 5)
                                nc.vector.tensor_copy(probT[:, m % 3].rearrange("p a k -> p (a k)")[:, 0:width],
                                                      t_ps[:, m % 3, 0:width]).then_inc(pt_done, 1)

            @block.scalar
            def _(act):
                with act.Fori(0, NG // 2) as i:
                    for u in range(2):
                        g = 2 * i + u
                        for n in range(NU + 5):
                            if n < NU:
                                c, x, b = units[n]
                                act.wait_ge(p_done, NU * g + n + 4)
                                for y in range(2):
                                    m = P * block_keys(c, b + y)[2]
                                    pr = prob[:, n % 4, y, 2 * P - m:]
                                    st = stage[:, stage_slot(u, c), b + y, x]
                                    ins = nc.scalar.activation(pr, pr, ACT.Exp, bias=st[:, DA + 1:DA + 2], scale=-1.0,
                                                               accum_out=st[:, DA:DA + 1])
                                ins.then_inc(e_done, 1)
                            m = n - 5
                            if m >= 0 and m % 4 == 3:
                                c, x, b = units[m - 3]
                                act.wait_ge(pv_done, NU * g + m + 4)
                                nc.scalar.activation(stage[:, stage_slot(u, c), b:b + 8, x, 0:DA],
                                                     o_ps[:, (m // 4) % 2].rearrange("p (b d) -> p b d", d=DA),
                                                     ACT.Copy).then_inc(o_out, 1)

            @block.tensor
            def _(pe):
                pe.wait_ge(const, 16)
                pe.sem_inc(t_done, 4)
                pe.sem_inc(pv_done, 3)
                with pe.Fori(0, NG // 2) as i:
                    for u in range(2):
                        g = 2 * i + u
                        pe.wait_ge(landed[u], 16 * NLD * (i + 1))
                        for n in range(NU + 4):
                            if n < NU:
                                c, x, b = units[n]
                                r, d = slice(x * DA, (x + 1) * DA), DILS[c]
                                pe.wait_ge(p_done, NU * g + n + 1)
                                for y in range(2):
                                    q0, k0, m = block_keys(c, b + y)
                                    mm = pe.matmul(s_ps[:, n % 3, y * 2 * P + (2 - m) * P:(y + 1) * 2 * P],
                                                   qT[r, u, q0:q0 + d * (P - 1) + 1:d],
                                                   kT[r, u, k0:k0 + d * (m * P - 1) + 1:d], start=True, stop=True)
                                mm.then_inc(s_done, 1)
                            if 2 <= n < NU + 2:
                                m = n - 2
                                c, x, b = units[m]
                                pe.wait_ge(e_done, NU * g + m + 1)
                                pe.wait_ge(pt_done, NU * g + m + 1)
                                for a, (y, _, place) in enumerate(tiles(c, b)):
                                    mm = pe.transpose(t_ps[:, m % 3, a * P:(a + 1) * P],
                                                      prob[:, m % 4, y, place * P:(place + 1) * P], ident[:])
                                mm.then_inc(t_done, 1)
                            if n >= 4:
                                m = n - 4
                                c, x, b = units[m]
                                pe.wait_ge(pt_done, NU * g + m + 4)
                                if m % 4 == 0:
                                    pe.wait_ge(o_out, NGRP * g + m // 4 + 1)
                                ts = tiles(c, b)
                                for a, (y, vt, _) in enumerate(ts):
                                    col = (2 * (m % 4) + y) * DA
                                    mm = pe.matmul(o_ps[:, (m // 4) % 2, col:col + DA], probT[:, m % 3, a],
                                                   v[:, u, c, vt, x * DA:(x + 1) * DA],
                                                   start=(a == 0 or ts[a - 1][0] != y),
                                                   stop=(a == len(ts) - 1 or ts[a + 1][0] != y))
                                mm.then_inc(pv_done, 1)


def attention_sample(nc, projT, projN, cache_kT, cache_v, rep_d, ident_d, attn_s):
    FAR = WIN - 512
    NA = FAR // 2
    NK = NA + NT + (WIN - FAR)
    NPAIR = NB // 2
    MW = 16
    NM = FAR // MW
    ktiles = ([slice(a, NA, NT) for a in range(NT)] + [slice(NA, NA + NT)]
              + [slice(NA + NT + a * P, NA + NT + (a + 1) * P) for a in range((WIN - FAR) // P)])
    rows_of = [NM] * NT + [NT] + [P] * ((WIN - FAR) // P)
    NKT = len(ktiles)
    with ExitStack() as ctx:
        sb, ps, sem = region(ctx, nc)
        ident = sb("d_ident", [P, P])
        kc = sb("d_kc", [P, 2, NG, WIN])
        vfar, vnear = sb("d_vfar", [NM, 2, NT, WA]), sb("d_vnear", [P, 2, (WIN - FAR) // P, WA])
        vn = sb("d_vn", [NT, 2, WA])
        qs, ks = sb("d_qs", [P, NG, TS]), sb("d_ks", [P, NG, TS])
        qb = sb("d_qb", [P, NG, 2, TS])
        kn = sb("d_kn", [P, 2, NG, NT])
        bias = sb("d_bias", [P, WIN + NT])
        prob, probT = sb("d_prob", [P, NK]), sb("d_probT", [P, NKT, P])
        mn, nm, den = sb("d_mn", [P, 4]), sb("d_nm", [P, 1]), sb("d_den", [P, 1])
        aT, an = sb("d_aT", [P, NG, TS]), sb("d_an", [TS, WA])
        s_ps, t_ps, o_ps = ps("d_s_ps", [P, 3, 512]), ps("d_t_ps", [P, 4, 512]), ps("d_o_ps", [P, 2, NG, 2 * NT])
        k_landed, v_landed = [sem(f"d_k_landed{u}") for u in range(2)], [sem(f"d_v_landed{u}") for u in range(2)]
        const, zeroed, q_done, qk_done, turn, min_done = (sem(f"d_{n}") for n in ("const", "zeroed", "q_done", "qk_done", "turn", "min_done"))
        e_done, r_done, p_done, t_done, pt_done, pv_done, o_done, f_done, stored = (
            sem(f"d_{n}") for n in ("e_done", "r_done", "p_done", "t_done", "pt_done", "pv_done", "o_done", "f_done", "stored"))
        nm_done = sem("d_nm_done")
        NV = 3
        with nc.Block() as block:
            @block.sync
            def _(sp):
                sp.dma_start(ident[:], ident_d).then_inc(const, 16)
                sp.dma_start(qs[:], projT[0:NG, :, T:TT].rearrange("g p t -> p g t")).then_inc(const, 16)
                sp.dma_start(ks[:], projT[NG:2 * NG, :, T:TT].rearrange("g p t -> p g t")).then_inc(const, 16)
                for u in range(2):
                    for h in range(HA):
                        src = bass.AP(tensor=rep_d.tensor, offset=h * LD + NT - 1, ap=[[HA * LD - 1, NT], [1, WIN + NT]])
                        sp.dma_start(bias[(u * HA + h) * NT:(u * HA + h + 1) * NT, :], src).then_inc(const, 16)
                for s in range(NB):
                    i, u = s // 2, s % 2
                    if i:
                        sp.wait_ge(qk_done, 2 * (i - 1) + u + 3)
                    sp.dma_start(kc[:, u], cache_kT[s].rearrange("(g p) n -> p g n", p=P)).then_inc(k_landed[u], 16)
                    if i:
                        sp.wait_ge(pv_done, 2 * (i - 1) + u + 1)
                    sp.dma_start(vfar[:, u], cache_v[s, 0:FAR, :].rearrange("(m r) d -> m r d", r=MW)[:, 0:NT, :]
                                 ).then_inc(v_landed[u], 16)
                    sp.dma_start(vnear[:, u], cache_v[s, FAR:WIN, :].rearrange("(a p) d -> p a d", p=P)
                                 ).then_inc(v_landed[u], 16)
                    sp.dma_start(vn[:, u], projN[T + s * NT:T + (s + 1) * NT, 0:WA]).then_inc(v_landed[u], 16)
                sp.wait_ge(f_done, 2)
                sp.dma_start(attn_s, an[:]).then_inc(stored, 16)
                sp.wait_ge(stored, 16)

            @block.gpsimd
            def _(pool):
                nc.gpsimd.memset(qb[:], 0.0).then_inc(zeroed, 1)

            @block.vector
            def _(dve):
                dve.wait_ge(zeroed, 1)
                dve.wait_ge(const, 16 * (3 + 2 * HA))
                with dve.Fori(0, NPAIR) as i:
                    dve.wait_ge(qk_done, 2 * i + 2)
                    for u in range(2):
                        c = bass.ds((2 * i + u) * NT, NT)
                        for x in range(2):
                            r = slice(x * DA, (x + 1) * DA)
                            for g in range(NG):
                                col = (2 * g + x) * NT
                                nc.vector.tensor_copy(qb[r, g, u, col:col + NT], qs[r, g, c])
                        ins = nc.vector.tensor_copy(kn[:, u], ks[:, :, c])
                    ins.then_inc(q_done, 1)
                    dve.wait_ge(t_done, i + 1)
                    dve.wait_ge(qk_done, 2 * i + 4)
                    dve.sem_inc(turn, 1)
                    far = bias[:, 0:FAR].rearrange("p (m r) -> p m r", r=MW)[:, :, 0:NT]
                    cut = lambda ap: ap.rearrange("p (m r) -> p m r", r=NT)
                    parts = ((cut(prob[:, 0:512]), cut(s_ps[:, 0, :]), far[:, 0:64]),
                             (cut(prob[:, 512:NA]), cut(s_ps[:, 1, 0:NA - 512]), far[:, 64:96]),
                             (prob[:, NA:NA + NT], s_ps[:, 1, NA - 512:NA - 512 + NT], bias[:, WIN:WIN + NT]),
                             (prob[:, NA + NT:NK], s_ps[:, 2, :], bias[:, FAR:WIN]))
                    for n, (out, s, bb) in enumerate(parts):
                        ins = nc.vector.tensor_tensor_reduce(out, s, bb, -SCALE, 3e38, ALU.add, ALU.min, mn[:, n:n + 1])
                    ins.then_inc(min_done, 1)
                    dve.wait_ge(min_done, i + 1)
                    nc.vector.tensor_reduce(nm[:], mn[:], AX, ALU.min).then_inc(nm_done, 1)
                    dve.wait_ge(e_done, i + 1)
                    nc.vector.reciprocal(den[:], den[:]).then_inc(r_done, 1)
                    dve.wait_ge(r_done, i + 1)
                    nc.vector.tensor_scalar(prob[:], prob[:], den[:, 0:1], None, ALU.mult).then_inc(p_done, 1)
                    dve.wait_ge(pv_done, 2 * i + 2)
                    for u in range(2):
                        c = bass.ds((2 * i + u) * NT, NT)
                        for x in range(2):
                            r = slice(x * DA, (x + 1) * DA)
                            ins = nc.vector.tensor_copy(aT[r, :, c], o_ps[r, u, :, x * NT:(x + 1) * NT])
                    ins.then_inc(o_done, 1)
                dve.wait_ge(f_done, 1)
                nc.vector.tensor_copy(an[:], t_ps[0:TS, 0, :]).then_inc(f_done, 1)

            @block.scalar
            def _(act):
                with act.Fori(0, NPAIR) as i:
                    act.wait_ge(nm_done, i + 1)
                    nc.scalar.activation(prob[:], prob[:], ACT.Exp, bias=nm[:, 0:1], scale=-1.0,
                                         accum_out=den[:, 0:1]).then_inc(e_done, 1)
                    act.wait_ge(t_done, i + 2)
                    for t0, t1 in ((0, 4), (4, 8), (8, 9), (9, 12), (12, 13)):
                        w, c = rows_of[t0], (t0 % 4) * P
                        ins = nc.scalar.activation(probT[0:w, t0:t1].rearrange("p a k -> p (a k)"),
                                                   t_ps[0:w, t0 // 4, c:c + (t1 - t0) * P], ACT.Copy)
                    ins.then_inc(pt_done, 1)

            @block.tensor
            def _(pe):
                pe.sem_inc(t_done, 1)
                pe.sem_inc(qk_done, 2)
                pe.wait_ge(const, 16 * (3 + 2 * HA))
                with pe.Fori(0, NPAIR) as i:
                    pe.wait_ge(q_done, i + 1)
                    for u in range(2):
                        pe.wait_ge(k_landed[u], 16 * (i + 1))
                        o = slice(u * TS, (u + 1) * TS)
                        far = lambda g, a: kc[:, u, g, a * 512:(a + 1) * 512].rearrange("p (m r) -> p m r", r=MW)[:, :, 0:NT]
                        cut = lambda ap: ap.rearrange("p (m r) -> p m r", r=NT)
                        parts = [(cut(s_ps[o, 0, 0:256]), lambda g: far(g, 0)), (cut(s_ps[o, 0, 256:512]), lambda g: far(g, 1)),
                                 (cut(s_ps[o, 1, 0:256]), lambda g: far(g, 2)), (s_ps[o, 1, 256:256 + NT], lambda g: kn[:, u, g]),
                                 (s_ps[o, 2, :], lambda g: kc[:, u, g, FAR:WIN])]
                        for out, rhs in parts:
                            for g in range(NG):
                                mm = pe.matmul(out, qb[:, g, u], rhs(g), start=(g == 0), stop=(g == NG - 1))
                        mm.then_inc(qk_done, 1)
                    pe.wait_ge(p_done, i + 1)
                    for a, cols in enumerate(ktiles):
                        mm = pe.transpose(t_ps[0:rows_of[a], a // 4, (a % 4) * P:(a % 4 + 1) * P], prob[:, cols], ident[:])
                    mm.then_inc(t_done, 1)
                    pe.wait_ge(pt_done, i + 1)
                    for u in range(2):
                        pe.wait_ge(v_landed[u], 16 * NV * (i + 1))
                        for g in range(NG):
                            d = slice(g * P, (g + 1) * P)
                            values = ([vfar[:, u, a, d] for a in range(NT)] + [vn[:, u, d]]
                                      + [vnear[:, u, a, d] for a in range((WIN - FAR) // P)])
                            for a, vv in enumerate(values):
                                col = u * TS + g * 2 * NT
                                mm = pe.matmul(o_ps[:, u, g], vv, probT[0:rows_of[a], a, col:col + 2 * NT],
                                               start=(a == 0), stop=(a == NKT - 1))
                        mm.then_inc(pv_done, 1)
                pe.wait_ge(o_done, NPAIR)
                for g in range(NG):
                    mm = pe.transpose(t_ps[0:TS, 0, g * P:(g + 1) * P], aT[:, g], ident[:])
                mm.then_inc(f_done, 1)


def merge_and_project(nc, x_all, partials, attn_s, projN, o_b, w_o, norm_g, ln_g, ln_b, ident_d, y):
    NTL = T // P
    H = 512
    with ExitStack() as ctx:
        sb, ps, sem = region(ctx, nc)
        ident = sb("m_ident", [P, P])
        wraw = sb("m_wraw", [P, 2, D])
        whi, wlo = sb("m_whi", [P, KD, D], F32R), sb("m_wlo", [P, KD, D], F32R)
        ngb, lgb, lbb = sb("m_ngb", [P, WB]), sb("m_lgb", [P, D]), sb("m_lbb", [P, D])
        half = sb("m_half", [P, HB])
        xt = sb("m_x", [P, 4, D])
        pt = sb("m_part", [P, 2, NC, HA, OW])
        gate, ob = sb("m_gate", [P, 2, 2, H]), sb("m_ob", [P, 2, H])
        mn, wexp, wd, dsum = sb("m_mn", [P, HA]), sb("m_wexp", [P, NC, HA]), sb("m_wd", [P, NC, HA]), sb("m_dsum", [P, HA])
        mixa = sb("m_mixa", [TS, H])
        sq, ms, rs = sb("m_sq", [P, H]), sb("m_ms", [P, HB]), sb("m_rs", [P, HB])
        mix = sb("m_mix", [P, D])
        mhi, mlo = sb("m_mhi", [P, 2, KD, P], F32R), sb("m_mlo", [P, 2, KD, P], F32R)
        z = sb("m_z", [P, D])
        st, mv, vr, rstd, nb = sb("m_st", [P, 2, 6]), sb("m_mv", [P, 2]), sb("m_vr", [P, 1]), sb("m_rstd", [P, 1]), sb("m_nb", [P, 1])
        yt = sb("m_y", [P, 2, D])
        t_ps, z_ps = ps("m_t_ps", [P, 2, H]), ps("m_z_ps", [P, 2, 2, H])
        const, w_hi, w_lo = sem("m_const"), sem("m_w_hi"), sem("m_w_lo")
        w_landed, landed, y_free = ([sem(f"m_{n}{u}") for u in range(2)] for n in ("w_landed", "landed", "y_free"))
        chain, d_done, wexp_done, ms_done, rs_done, mix_done = (sem(f"m_{n}") for n in ("chain", "d_done", "wexp_done", "ms_done", "rs_done", "mix_done"))
        t_done, mhi_done, mlo_done, z_done, vr_done, rstd_done, nb_done, n_done, y_done, zr = (
            sem(f"m_{n}") for n in ("t_done", "mhi_done", "mlo_done", "z_done", "vr_done", "rstd_done", "nb_done", "n_done", "y_done", "zr"))
        y_mul, turn_dve, turn_sp = sem("m_y_mul"), sem("m_turn_dve"), sem("m_turn_sp")
        half_set = sem("m_half_set")
        x_landed = [sem(f"m_x_landed{w}") for w in range(4)]
        NLD = 4

        def run(eng, step):
            for t in range(4):
                step(t, 0, t, P, P if t >= 1 else 0, P if t >= 2 else 0)
            with eng.Fori(1, NTL // 4) as i:
                for v in range(4):
                    step(4 * i + v, i, v, P, P, P)
            step(NTL, NTL // 4, 0, TS, P, P)
            step(NTL + 1, NTL // 4, 1, 0, TS, P)
            step(NTL + 2, NTL // 4, 2, 0, 0, TS)

        with nc.Block() as block:
            @block.sync
            def _(sp):
                def load(t, u, v, n=P, sample=False):
                    rows = bass.ds(t * P, n)
                    sp.dma_start(xt[0:n, v], x_all[rows, :]).then_inc(x_landed[v], 16)
                    if sample:
                        sp.dma_start(mixa[0:n, :], attn_s).then_inc(landed[u], 16)
                    else:
                        sp.dma_start(pt[0:n, u], partials[:, rows, :, :].rearrange("c p h w -> p c h w")).then_inc(landed[u], 16)
                    sp.dma_start(gate[0:n, u, 0], projN[rows, WA:2 * WA]).then_inc(landed[u], 16)
                    sp.dma_start(gate[0:n, u, 1], projN[rows, 3 * WA:4 * WA]).then_inc(landed[u], 16)
                    sp.dma_start(ob[0:n, u], o_b[rows, :]).then_inc(landed[u], 16)

                def store(t, u, n=P):
                    sp.wait_ge(y_done, t + 1)
                    sp.sem_inc(turn_sp, 1)
                    sp.dma_start(y[bass.ds(t * P, n), :], yt[0:n, u]).then_inc(y_free[u], 16)

                for u in range(2):
                    sp.sem_inc(y_free[u], 16)
                sp.dma_start(ident[:], ident_d).then_inc(const, 16)
                for dst, src in ((lgb[:], ln_g), (lbb[:], ln_b)):
                    sp.dma_start(dst, src[0:1, :].to_broadcast([P, D])).then_inc(const, 16)
                for h in range(HB):
                    sp.dma_start(ngb[:, h * DB:(h + 1) * DB], norm_g[0:1, :].to_broadcast([P, DB])).then_inc(const, 16)
                load(0, 0, 0)
                load(1, 1, 1)
                for k in range(KD):
                    if k >= 2:
                        sp.wait_ge(w_lo, k - 1)
                    sp.dma_start(wraw[:, k % 2], w_o[:, k, :]).then_inc(w_landed[k % 2], 16)
                def step(t, v, n, sample=False):
                    sp.wait_ge(mix_done, t + 1)
                    if not (isinstance(t, int) and t < 2):
                        sp.sem_inc(turn_sp, 1)
                        sp.wait_ge(zr, t - 1)
                    sp.sem_inc(turn_sp, 1)
                    load(t + 2, v % 2, (v + 2) % 4, n, sample)
                step(0, 0, P)
                step(1, 1, P)
                step(2, 2, P)
                store(0, 0)
                step(3, 3, P)
                store(1, 1)
                with sp.Fori(1, NTL // 4 - 1) as i:
                    for v in range(4):
                        step(4 * i + v, v, P)
                        store(4 * i + v - 2, v % 2)
                for t in range(NTL - 4, NTL - 2):
                    step(t, t % 4, P)
                    store(t - 2, t % 2)
                step(NTL - 2, 2, TS, True)
                store(NTL - 4, 0)
                for t in range(NTL - 3, NTL):
                    store(t, t % 2)
                store(NTL, 0, TS)
                for u in range(2):
                    sp.wait_ge(y_free[u], 16 * (NTL // 2 + 2 - u))

            @block.vector
            def _(dve):
                tt = nc.vector.tensor_tensor
                nc.vector.memset(half[:], -0.5).then_inc(half_set, 1)
                for k in range(KD):
                    dve.wait_ge(w_hi, k + 1)
                    tt(wlo[:, k], wraw[:, k % 2], whi[:, k].bitcast(F32), ALU.subtract).then_inc(w_lo, 1)
                dve.wait_ge(const, 16 * 7)

                CF, CFS, CB = 14, 5, 2

                def step(t, i, v, nf, nm_, nbk):
                    u, turn = v % 2, 2 * i + v // 2
                    sample = nf == TS
                    if isinstance(t, int):
                        base = sum(CF if s < NTL else (CFS if s == NTL else 0) for s in range(t)) + CB * max(t - 2, 0)
                    else:
                        base = (CF + CB) * t - 2 * CB
                    link = [0]

                    def then(ins):
                        link[0] += 1
                        ins.then_inc(chain, 1)
                        dve.wait_ge(chain, base + link[0])

                    if nf:
                        dve.wait_ge(landed[u], 16 * NLD * (turn + 1))
                        r = slice(0, nf)
                        a = mix[r, 0:H]
                        if isinstance(t, int) and t == 0:
                            pass
                        else:
                            dve.wait_ge(t_done, t)
                        if not sample:
                            nmx = pt[r, u, :, :, DA + 1]
                            then(tt(mn[r], nmx[:, 0], nmx[:, 1], ALU.min))
                            then(tt(mn[r], mn[r], nmx[:, 2], ALU.min))
                            tt(wd[r], mn[r].unsqueeze(1).to_broadcast([nf, NC, HA]), nmx, ALU.subtract).then_inc(d_done, 1)
                        o = ob[r, u]
                        if sample:
                            then(tt(a, mixa[r], gate[r, u, 0], ALU.mult))
                        then(tt(sq[r], o, o, ALU.mult))
                        then(nc.vector.tensor_reduce(ms[r], sq[r].rearrange("p (h v) -> p h v", h=HB), AX, ALU.add))
                        nc.vector.tensor_scalar(ms[r], ms[r], 1.0 / DB, EPS, ALU.mult, ALU.add).then_inc(ms_done, 1)
                        if not sample:
                            dve.wait_ge(wexp_done, t + 1)
                            then(tt(wd[r], wexp[r], pt[r, u, :, :, DA], ALU.mult))
                            then(tt(dsum[r], wd[r, 0], wd[r, 1], ALU.add))
                            then(tt(dsum[r], dsum[r], wd[r, 2], ALU.add))
                            then(nc.vector.reciprocal(dsum[r], dsum[r]))
                            then(tt(wexp[r], wexp[r], dsum[r].unsqueeze(1).to_broadcast([nf, NC, HA]), ALU.mult))
                            po = pt[r, u].rearrange("p c h w -> p (c h) w")[:, :, 0:DA]
                            wv = wexp[r].rearrange("p c h -> p (c h)").unsqueeze(2).to_broadcast([nf, NC * HA, DA])
                            then(tt(po, po, wv, ALU.mult))
                            av = a.rearrange("p (h d) -> p h d", h=HA)
                            then(tt(av, pt[r, u, 0, :, 0:DA], pt[r, u, 1, :, 0:DA], ALU.add))
                            then(tt(av, av, pt[r, u, 2, :, 0:DA], ALU.add))
                            tt(a, a, gate[r, u, 0], ALU.mult)
                        bpart = mix[r, H:D]
                        then(tt(gate[r, u, 1], gate[r, u, 1], ngb[r], ALU.mult))
                        dve.wait_ge(rs_done, t + 1)
                        then(tt(o.rearrange("p (h v) -> p h v", h=HB), o.rearrange("p (h v) -> p h v", h=HB),
                                rs[r].unsqueeze(2).to_broadcast([nf, HB, DB]), ALU.mult))
                        tt(bpart, o, gate[r, u, 1], ALU.mult).then_inc(mix_done, 1)
                        want = CFS if sample else CF
                        assert link[0] == want, (link[0], want)
                    if nbk:
                        r = slice(0, nbk)
                        dve.wait_ge(x_landed[(v + 2) % 4], 16 * (i + 1 if v >= 2 else i))
                        dve.wait_ge(z_done, t - 1)
                        if not (isinstance(t, int) and t < 3):
                            dve.wait_ge(n_done, t - 2)
                        for g in range(2):
                            c = slice(g * H, (g + 1) * H)
                            ins = nc.vector.scalar_tensor_tensor(z[r, c], xt[r, (v + 2) % 4, c], ALPHA,
                                                                 z_ps[r, u, g], ALU.mult, ALU.add)
                        ins.then_inc(zr, 1)
                        dve.wait_ge(zr, t - 1)
                        for g in range(2):
                            ins = nc.vector.bn_stats(st[r, g], z[r, g * H:(g + 1) * H])
                        then(ins)
                        dve.sem_inc(turn_dve, 1)
                        then(nc.vector.bn_aggr(mv[r], st[r].rearrange("p a b -> p (a b)")))
                        nc.vector.tensor_scalar(vr[r], mv[r, 1:2], EPS, None, ALU.add).then_inc(vr_done, 1)
                    if nf:
                        dve.wait_ge(mhi_done, t + 1)
                        if not (isinstance(t, int) and t < 2):
                            dve.wait_ge(z_done, t - 1)
                        r = slice(0, nf)
                        for g in range(2):
                            k = slice(4 * g, 4 * g + 4)
                            ins = tt(mlo[:, u, k, 0:nf], t_ps[:, g].rearrange("p (k n) -> p k n", k=4)[:, :, 0:nf],
                                     mhi[:, u, k, 0:nf].bitcast(F32), ALU.subtract)
                        ins.then_inc(mlo_done, 1)
                    if nbk:
                        r = slice(0, nbk)
                        dve.wait_ge(rstd_done, t - 1)
                        nc.vector.scalar_tensor_tensor(nb[r], mv[r, 0:1], -1.0, rstd[r], ALU.mult, ALU.mult).then_inc(nb_done, 1)
                        dve.wait_ge(n_done, t - 1)
                        tt(yt[r, u], yt[r, u], lgb[r], ALU.mult).then_inc(y_mul, 1)

                run(dve, step)

            @block.scalar
            def _(act):
                for k in range(KD):
                    act.wait_ge(w_landed[k % 2], 16 * (k // 2 + 1))
                    nc.scalar.activation(whi[:, k], wraw[:, k % 2], ACT.Copy).then_inc(w_hi, 1)

                def step(t, i, v, nf, nm_, nbk):
                    u, turn = v % 2, 2 * i + v // 2
                    if nf == P:
                        act.wait_ge(d_done, t + 1)
                        nc.scalar.activation(wexp[:], wd[:], ACT.Exp).then_inc(wexp_done, 1)
                    if nf:
                        act.wait_ge(t_done, t + 1)
                        if not (isinstance(t, int) and t < 2):
                            act.wait_ge(z_done, t - 1)
                        for g in range(2):
                            ins = nc.scalar.activation(mhi[:, u, 4 * g:4 * g + 4, 0:nf],
                                                       t_ps[:, g].rearrange("p (k n) -> p k n", k=4)[:, :, 0:nf], ACT.Copy)
                        ins.then_inc(mhi_done, 1)
                    if nbk:
                        r = slice(0, nbk)
                        act.wait_ge(nb_done, t - 1)
                        act.wait_ge(y_free[u], 16 * turn)
                        nc.scalar.activation(yt[r, u], z[r], ACT.Identity, bias=nb[r, 0:1], scale=rstd[r, 0:1]).then_inc(n_done, 1)
                run(act, step)

            @block.gpsimd
            def _(pool):
                pool.wait_ge(half_set, 1)

                def step(t, i, v, nf, nm_, nbk):
                    u, turn = v % 2, 2 * i + v // 2
                    if nf:
                        r = slice(0, nf)
                        pool.wait_ge(ms_done, t + 1)
                        nc.gpsimd.tensor_tensor(rs[r], ms[r], half[r], ALU.pow).then_inc(rs_done, 1)
                    if nbk:
                        r = slice(0, nbk)
                        pool.wait_ge(vr_done, t - 1)
                        nc.gpsimd.tensor_tensor(rstd[r], vr[r], half[r, 0:1], ALU.pow).then_inc(rstd_done, 1)
                        pool.wait_ge(y_mul, t - 1)
                        nc.gpsimd.tensor_tensor(yt[r, u], yt[r, u], lbb[r], ALU.add).then_inc(y_done, 1)
                run(pool, step)

            @block.tensor
            def _(pe):
                pe.wait_ge(const, 16 * 7)
                pe.wait_ge(w_lo, KD)

                def step(t, i, v, nf, nm_, nbk):
                    u, turn = v % 2, 2 * i + v // 2
                    if nf:
                        pe.wait_ge(mix_done, t + 1)
                        if not (isinstance(t, int) and t < 1):
                            pe.wait_ge(mlo_done, t)
                        for k in range(KD):
                            mm = pe.transpose(t_ps[:, k // 4, (k % 4) * P:(k % 4) * P + nf], mix[0:nf, k * P:(k + 1) * P],
                                              ident[0:nf, 0:nf])
                        mm.then_inc(t_done, 1)
                    if nm_:
                        w = 1 - u
                        pe.wait_ge(mlo_done, t)
                        if not (isinstance(t, int) and t < 3):
                            pe.wait_ge(zr, t - 2)
                        for k in range(KD):
                            for a, (m, ww) in enumerate(((mhi, whi), (mhi, wlo), (mlo, whi))):
                                for g in range(2):
                                    mm = pe.matmul(z_ps[0:nm_, w, g], m[:, w, k, 0:nm_], ww[:, k, g * H:(g + 1) * H],
                                                   start=(k == 0 and a == 0), stop=(k == KD - 1 and a == 2))
                        mm.then_inc(z_done, 1)
                run(pe, step)


def build(nc, a, o):
    dram = lambda name, shape: nc.dram_tensor(name, shape, F32, kind="Internal").ap()
    projT = dram("projT", [NCT, P, TT])
    projN = dram("projN", [TT, WN])
    project_transposed(nc, a["xT"], a["w_t"], projT, a["cache_kT"], a["cache_v"], o["kwin_s"], o["vwin_s"])
    project_natural(nc, a["xT"], a["w_n"], projT, projN, o["kwin_p"], o["vwin_p"], o["kwin_s"], o["vwin_s"])
    rep_p, rep_d = dram("rep_p", [P, HA, NC * LB]), dram("rep_d", [NT, HA, LD])
    o_b = dram("o_b", [TT, WB])
    bias_vectors(nc, a["rel_bias"], a["expand"], rep_p, rep_d)
    hgrn_prompt(nc, projT, projN, a["lbT"], a["go_on"], a["lmask"], a["dmask"], a["ident"], o_b, o["hgrn_p"])
    hgrn_sample(nc, projT, projN, a["lbT"], a["go_on_s"], a["smask"], a["rowm"], a["ident"], a["state"], o_b, o["hgrn_s"])
    partials = dram("partials", [NC, T, HA, OW])
    attn_s = dram("attn_s", [TS, WA])
    attention_prompt(nc, projT, projN, rep_p, a["ident"], partials)
    attention_sample(nc, projT, projN, a["cache_kT"], a["cache_v"], rep_d, a["ident"], attn_s)
    merge_and_project(nc, a["x"], partials, attn_s, projN, o_b, a["w_o"], a["norm_g"], a["ln_g"], a["ln_b"], a["ident"], o["y"])


def kernel(x_prompt, x_sample, cache_k, cache_v, state_hgrn, w_in, w_out, rel_bias, lb_param, hgrn_norm_g,
           ln_g, ln_b):
    import concourse.bacc as bacc
    from concourse.bass_utils import run_bass_kernel_spmd

    A = np.asarray
    x_all = np.concatenate([A(x_prompt).reshape(T, D), A(x_sample).reshape(TS, D)])
    w = A(w_in)[0].reshape(KD, P, 8, 512)
    arrays = {
        "x": x_all,
        "xT": x_all.T.reshape(KD, P, TT).transpose(1, 0, 2),
        "w_t": w[:, :, [0, 1, 4, 5]].reshape(KD, P, NCT, P).transpose(2, 1, 0, 3),
        "w_n": w[:, :, [2, 3, 6, 7]].reshape(KD, P, WN).transpose(1, 0, 2),
        "cache_kT": A(cache_k)[0].transpose(0, 2, 3, 1).reshape(NB, WA, WIN),
        "cache_v": A(cache_v)[0].reshape(NB, WIN, WA),
        "state": A(state_hgrn)[0],
        "w_o": A(w_out)[0].reshape(KD, P, D).transpose(1, 0, 2),
        "rel_bias": A(rel_bias),
        "lbT": A(lb_param).reshape(2, HB, P).transpose(2, 0, 1),
        "norm_g": A(hgrn_norm_g), "ln_g": A(ln_g), "ln_b": A(ln_b),
        **shape_constants(),
    }
    outs = {
        "y": [TT, D], "kwin_p": [NG, P, T], "vwin_p": [T, WA],
        "kwin_s": [NB, WA, WIN], "vwin_s": [NB, WIN, WA],
        "hgrn_p": [HB, DB, DB], "hgrn_s": [NB, HB, DB, DB],
    }
    nc = bacc.Bacc("TRN2", target_bir_lowering=False, num_devices=1)
    arrays = {f"in_{k}": np.ascontiguousarray(v) for k, v in arrays.items()}
    ins = {k[3:]: nc.dram_tensor(k, v.shape, mybir.dt.from_np(v.dtype), kind="ExternalInput").ap()
           for k, v in arrays.items()}
    outp = {k: nc.dram_tensor(f"out_{k}", s, F32, kind="ExternalOutput").ap() for k, s in outs.items()}
    build(nc, ins, outp)
    r = run_bass_kernel_spmd(nc, [arrays], core_ids=[0]).results[0]
    g = {k: r[f"out_{k}"] for k in outs}
    return (g["y"][:T].reshape(1, T, D), g["y"][T:].reshape(NB, NT, D),
            g["kwin_p"].reshape(1, 1, HA, DA, T).transpose(0, 1, 4, 2, 3), g["vwin_p"].reshape(1, 1, T, HA, DA),
            g["kwin_s"].reshape(1, NB, HA, DA, WIN).transpose(0, 1, 4, 2, 3),
            g["vwin_s"].reshape(1, NB, WIN, HA, DA),
            g["hgrn_p"].reshape(1, 1, HB, DB, DB), g["hgrn_s"].reshape(1, NB, HB, DB, DB))
```

```python
from contextlib import ExitStack

import numpy as np
import concourse.bass as bass
from concourse import mybir

F32 = mybir.dt.float32
F32R = mybir.dt.float32r
I32 = mybir.dt.int32
ALU = mybir.AluOpType
ACT = mybir.ActivationFunctionType
AX = mybir.AxisListType.X

P = 128
D = 1024
KD = D // P
T = 2048
NB, NT = 8, 8
TS = NB * NT
TT = T + TS
HA, DA = 8, 64
WA = HA * DA
NG = HA // 2
HB, DB = 4, 128
WB = HB * DB
WIN = 2048
DILS = (1, 4, 16)
NC = len(DILS)
BAND = 128
WROWS = WIN // (2 * NT)
BUCKETS, MAX_DIST = 32, 2048
SCALE = DA ** -0.5
ALPHA = 2.0 ** 0.25
EPS = 1e-5
NEG = -1e30

NCT = 16
WN = 2048
OW = DA + 2
CH = 64
SEG = 512
NSEG = T // SEG
SHIFTS = 6
NPR = SEG // P
LEVELS = (32, 16, 8, 4, 2, 1)
LB = 3 * BAND
LD = WIN + 2 * NT


def shape_constants():
    def buckets(dist):
        exact = BUCKETS // 2
        d = np.maximum(dist, 1).astype(np.float32)
        large = exact + (np.log(d / exact) / np.log(MAX_DIST / exact) * (BUCKETS - exact)).astype(np.int32)
        return np.where(dist < exact, dist, np.minimum(large, BUCKETS - 1)).astype(np.int32)

    expand = np.zeros((BUCKETS + 1, NC * LB + LD), np.float32)
    for c, dil in enumerate(DILS):
        for x in range(LB):
            sub = 2 * BAND - 1 - x
            if 0 <= sub <= BAND:
                expand[buckets(np.array([dil * sub]))[0], c * LB + x] = 1 / SCALE
            else:
                expand[BUCKETS, c * LB + x] = NEG
    for x in range(LD):
        dist = WIN + NT - 1 - x
        n = sum(dist >= 0 and dist % dil == 0 and dist // dil <= BAND for dil in DILS)
        if n:
            expand[buckets(np.array([dist]))[0], NC * LB + x] = 1 / SCALE
            expand[BUCKETS, NC * LB + x] = np.log(n) / SCALE
        else:
            expand[BUCKETS, NC * LB + x] = NEG

    def level(h, s, t):
        return (s // (2 * h) == t // (2 * h)) & (s % (2 * h) < h) & (t % (2 * h) >= h)

    def go_on(n, c):
        return np.tile((np.arange(n) % c != 0).astype(np.float32), (P, 1))

    s_of = np.arange(P)[:, None] % CH
    lmask = np.stack([level(h, s_of, (np.arange(CH // 2) // h * 2 * h + h + np.arange(CH // 2) % h)[None])
                      for h in LEVELS], 1)
    ss, st = np.arange(TS)[:, None], np.arange(TS)[None]
    smask = np.stack([level(h, ss, st) for h in LEVELS if h < NT] + [ss == st], 1)
    return {
        "expand": expand, "ident": np.eye(P, dtype=np.float32),
        "go_on": go_on(HB * SEG, CH), "go_on_s": go_on(HB * TS, NT),
        "lmask": lmask.astype(np.int32), "dmask": (s_of == np.arange(CH)[None]).astype(np.int32),
        "smask": smask.astype(np.int32),
        "rowm": (np.arange(TS)[:, None] // NT == np.arange(NB)[None]).astype(np.float32),
    }


def region(ctx, nc):
    def sb(name, shape, dt=F32):
        return ctx.enter_context(nc.sbuf_tensor(name, shape, dt))

    def ps(name, shape):
        return ctx.enter_context(nc.psum_tensor(name, shape, F32))

    def sem(name):
        return ctx.enter_context(nc.semaphore(name))
    return sb, ps, sem


def shift_window(eng, win, n, copied):
    b, (keys, old_keys, values, old_values) = n // 2, win
    if n % 2:
        half = WIN // 2
        eng.dma_start(values[b, 0:half, :], old_values[b, NT:half + NT, :]).then_inc(copied, 16)
        eng.dma_start(values[b, half:WIN - NT, :], old_values[b, half + NT:WIN, :]).then_inc(copied, 16)
    else:
        eng.dma_start(keys[b, :, 0], old_keys[b, :, 1]).then_inc(copied, 16)
        eng.dma_start(keys[b, :, 1, 0:WROWS - 1], old_keys[b, :, 0, 1:WROWS]).then_inc(copied, 16)


def project_transposed(nc, xT, w_t, projT):
    NCH = (TT + 511) // 512
    CW = (TT // NCH + 7) // 8 * 8
    chunks = [(j * CW, min(CW, TT - j * CW)) for j in range(NCH)]
    with ExitStack() as ctx:
        sb, ps, sem = region(ctx, nc)
        xhi, xlo = sb("xhi", [P, KD, TT], F32R), sb("xlo", [P, KD, TT], F32R)
        xraw = sb("xraw", [P, 2, KD * CW])
        wraw = sb("wraw", [P, 2, KD, P])
        whi, wlo = sb("whi", [P, 2, KD, P], F32R), sb("wlo", [P, 2, KD, P], F32R)
        stage = sb("stage", [P, 2, TT])
        acc = ps("acc", [P, NCH, 512])
        w_landed = [sem(f"w_landed{u}") for u in range(2)]
        x_landed = [sem(f"x_landed{u}") for u in range(2)]
        stage_free = [sem(f"stage_free{u}") for u in range(2)]
        w_hi, w_split = sem("w_hi"), sem("w_split")
        x_hi, x_split = sem("x_hi"), sem("x_split")
        chunk_done, bank_free = sem("chunk_done"), sem("bank_free")

        def xraw_of(j):
            n = chunks[j][1]
            return xraw[:, j % 2, 0:KD * n].rearrange("p (k n) -> p k n", k=KD)

        with nc.Block() as block:
            @block.sync
            def _(sp):
                for u in range(2):
                    sp.sem_inc(stage_free[u], 16)
                    sp.dma_start(wraw[:, u], w_t[u]).then_inc(w_landed[u], 16)
                for j, (c0, n) in enumerate(chunks):
                    if j >= 2:
                        sp.wait_ge(x_split, j - 1)
                    sp.dma_start(xraw_of(j), xT[:, :, c0:c0 + n]).then_inc(x_landed[j % 2], 16)

                def store(ct, u):
                    sp.wait_ge(bank_free, NCH * (ct + 2))
                    sp.dma_start(projT[ct], stage[:, u, :]).then_inc(stage_free[u], 16)

                with sp.Fori(0, NCT // 2 - 1) as i:
                    for u in range(2):
                        sp.wait_ge(w_split, 2 * i + u + 1)
                        sp.dma_start(wraw[:, u], w_t[2 * i + 2 + u]).then_inc(w_landed[u], 16)
                        store(2 * i + u, u)
                for u in range(2):
                    store(NCT - 2 + u, u)
                for u in range(2):
                    sp.wait_ge(stage_free[u], 16 * (NCT // 2 + 1))

            @block.vector
            def _(dve):
                def split_w(ct, u, i):
                    dve.wait_ge(w_landed[u], 16 * (i + 1))
                    nc.vector.tensor_copy(whi[:, u], wraw[:, u]).then_inc(w_hi, 1)
                    dve.wait_ge(w_hi, ct + 1)
                    nc.vector.tensor_tensor(wlo[:, u], wraw[:, u], whi[:, u].bitcast(F32),
                                            ALU.subtract).then_inc(w_split, 1)

                split_w(0, 0, 0)
                for j, (c0, n) in enumerate(chunks):
                    dve.wait_ge(x_hi, j + 1)
                    nc.vector.tensor_tensor(xlo[:, :, c0:c0 + n], xraw_of(j), xhi[:, :, c0:c0 + n].bitcast(F32),
                                            ALU.subtract).then_inc(x_split, 1)
                    if j == 0:
                        split_w(1, 1, 0)
                with dve.Fori(1, NCT // 2) as i:
                    for u in range(2):
                        dve.wait_ge(chunk_done, NCH * (2 * i + u - 1))
                        split_w(2 * i + u, u, i)

            @block.tensor
            def _(pe):
                with pe.Fori(0, NCT // 2) as i:
                    for u in range(2):
                        ct = 2 * i + u
                        pe.wait_ge(w_split, ct + 1)
                        for j, (c0, n) in enumerate(chunks):
                            pe.wait_ge(x_split, j + 1)
                            pe.wait_ge(bank_free, NCH * ct + j + 1)
                            for k in range(KD):
                                for a, (w, x) in enumerate(((whi, xhi), (whi, xlo), (wlo, xhi))):
                                    mm = pe.matmul(acc[:, j, 0:n], w[:, u, k], x[:, k, c0:c0 + n],
                                                   start=(k == 0 and a == 0), stop=(k == KD - 1 and a == 2))
                            mm.then_inc(chunk_done, 1)

            @block.scalar
            def _(act):
                act.sem_inc(bank_free, NCH)
                for j, (c0, n) in enumerate(chunks):
                    act.wait_ge(x_landed[j % 2], 16 * (j // 2 + 1))
                    nc.scalar.activation(xhi[:, :, c0:c0 + n], xraw_of(j), ACT.Copy).then_inc(x_hi, 1)
                for first, last, func in ((0, 4, ACT.Copy), (4, 6, ACT.Silu), (6, 8, ACT.Sigmoid)):
                    with act.Fori(first, last) as i:
                        for u in range(2):
                            act.wait_ge(stage_free[u], 16 * (i + 1))
                            for j, (c0, n) in enumerate(chunks):
                                act.wait_ge(chunk_done, NCH * (2 * i + u) + j + 1)
                                nc.scalar.activation(stage[:, u, c0:c0 + n], acc[:, j, 0:n],
                                                     func).then_inc(bank_free, 1)


def project_natural(nc, xT, w_n, projT, projN, kwin_p, vwin_p, kwin_s, vwin_s):
    NP = T // P // 2
    with ExitStack() as ctx:
        sb, ps, sem = region(ctx, nc)
        whi, wlo = sb("nwhi", [P, KD, WN], F32R), sb("nwlo", [P, KD, WN], F32R)
        wraw = sb("nwraw", [P, 2, WN])
        xraw = sb("nxraw", [P, 2, KD, P])
        xhi, xlo = sb("nxhi", [P, 2, KD, P], F32R), sb("nxlo", [P, 2, KD, P], F32R)
        stage = sb("nstage", [P, 2, WN])
        acc = ps("nacc", [P, 2, 4, 512])
        w_landed = [sem(f"nw_landed{u}") for u in range(2)]
        x_landed = [sem(f"nx_landed{u}") for u in range(2)]
        stage_free = [sem(f"nstage_free{u}") for u in range(2)]
        w_hi, w_split, x_hi, x_split = sem("nw_hi"), sem("nw_split"), sem("nx_hi"), sem("nx_split")
        tile_done, act_out, dve_out = sem("tile_done"), sem("act_out"), sem("dve_out")
        moved, v_out = sem("moved"), sem("v_out")

        with nc.Block() as block:
            @block.sync
            def _(sp):
                def load_x(t, u, n=P):
                    sp.dma_start(xraw[:, u, :, 0:n], xT[:, :, t:t + n] if isinstance(t, int) else
                                 xT[:, :, bass.ds(t, n)]).then_inc(x_landed[u], 16)

                def store(i, u, n=P):
                    sp.wait_ge(act_out, 2 * (2 * i + u) + 4 + 2)
                    sp.wait_ge(dve_out, 2 * (2 * i + u) + 4 + 2)
                    sp.dma_start(projN[bass.ds((2 * i + u) * P, n), :], stage[0:n, u, :]).then_inc(stage_free[u], 16)

                load_x(0, 0)
                for k in range(KD):
                    if k >= 2:
                        sp.wait_ge(w_split, k - 1)
                    sp.dma_start(wraw[:, k % 2], w_n[:, k, :]).then_inc(w_landed[k % 2], 16)
                    if k == 1:
                        load_x(P, 1)
                for u in range(2):
                    sp.sem_inc(stage_free[u], 16)
                with sp.Fori(0, NP - 1) as i:
                    for u in range(2):
                        sp.wait_ge(x_split, 2 * i + u + 1)
                        load_x((2 * i + 2 + u) * P, u)
                        store(i, u)
                sp.wait_ge(x_split, 2 * NP - 1)
                load_x(T, 0, TS)
                store(NP - 1, 0)
                store(NP - 1, 1)
                store(NP, 0, TS)
                for u in range(2):
                    sp.wait_ge(stage_free[u], 16 * (NP + 2 - u))

            @block.gpsimd
            def _(pool):
                for c in range(NG):
                    pool.dma_start(kwin_p[c], projT[NG + c, :, 0:T]).then_inc(moved, 16)
                    for b in range(NB):
                        pool.dma_start(kwin_s[b, c * P:(c + 1) * P, 1, WROWS - 1],
                                       projT[NG + c, :, T + b * NT:T + (b + 1) * NT]).then_inc(moved, 16)
                pool.wait_ge(moved, 16 * NG * (NB + 1))
                pool.wait_ge(stage_free[1], 16 * (NP + 1))
                pool.wait_ge(stage_free[0], 16 * (NP + 2))
                pool.dma_start(vwin_p, projN[0:T, 0:WA]).then_inc(v_out, 16)
                for b in range(NB):
                    pool.dma_start(vwin_s[b, WIN - NT:WIN, :],
                                   projN[T + b * NT:T + (b + 1) * NT, 0:WA]).then_inc(v_out, 16)
                pool.wait_ge(v_out, 16 * (NB + 1))

            @block.vector
            def _(dve):
                def split_x(t, i, u, n=P):
                    dve.wait_ge(x_landed[u], 16 * (i + 1))
                    nc.vector.tensor_copy(xhi[:, u, :, 0:n], xraw[:, u, :, 0:n]).then_inc(x_hi, 1)
                    dve.wait_ge(x_hi, t + 1)
                    nc.vector.tensor_tensor(xlo[:, u, :, 0:n], xraw[:, u, :, 0:n], xhi[:, u, :, 0:n].bitcast(F32),
                                            ALU.subtract).then_inc(x_split, 1)

                def evacuate(t, i, u, n=P):
                    dve.wait_ge(tile_done, t + 1)
                    dve.wait_ge(stage_free[u], 16 * (i + 1))
                    for g in (0, 2):
                        nc.vector.tensor_copy(stage[0:n, u, g * 512:(g + 1) * 512],
                                              acc[0:n, u, g, :]).then_inc(dve_out, 1)

                dve.sem_inc(dve_out, 4)
                split_x(0, 0, 0)
                for k in range(KD):
                    dve.wait_ge(w_landed[k % 2], 16 * (k // 2 + 1))
                    dve.wait_ge(w_hi, k + 1)
                    nc.vector.tensor_tensor(wlo[:, k], wraw[:, k % 2], whi[:, k].bitcast(F32),
                                            ALU.subtract).then_inc(w_split, 1)
                split_x(1, 0, 1)
                with dve.Fori(0, NP - 1) as i:
                    for u in range(2):
                        dve.wait_ge(tile_done, 2 * i + u + 1)
                        split_x(2 * i + 2 + u, i + 1, u)
                        evacuate(2 * i + u, i, u)
                dve.wait_ge(tile_done, 2 * NP - 1)
                split_x(2 * NP, NP, 0, TS)
                evacuate(2 * NP - 2, NP - 1, 0)
                evacuate(2 * NP - 1, NP - 1, 1)
                evacuate(2 * NP, NP, 0, TS)

            @block.tensor
            def _(pe):
                def tile(t, u, n=P, first=False):
                    pe.wait_ge(x_split, t + 1)
                    pe.wait_ge(dve_out, 2 * t + 2)
                    pe.wait_ge(act_out, 2 * t + 2)
                    for k in range(KD):
                        if first:
                            pe.wait_ge(w_split, k + 1)
                        for a, (x, w) in enumerate(((xhi, whi), (xhi, wlo), (xlo, whi))):
                            for g in range(4):
                                mm = pe.matmul(acc[0:n, u, g, :], x[:, u, k, 0:n], w[:, k, g * 512:(g + 1) * 512],
                                               start=(k == 0 and a == 0), stop=(k == KD - 1 and a == 2))
                    mm.then_inc(tile_done, 1)

                tile(0, 0, first=True)
                tile(1, 1)
                with pe.Fori(1, NP) as i:
                    for u in range(2):
                        tile(2 * i + u, u)
                tile(2 * NP, 0, TS)

            @block.scalar
            def _(act):
                act.sem_inc(act_out, 4)
                for k in range(KD):
                    act.wait_ge(w_landed[k % 2], 16 * (k // 2 + 1))
                    nc.scalar.activation(whi[:, k], wraw[:, k % 2], ACT.Copy).then_inc(w_hi, 1)

                def evacuate(t, i, u, n=P):
                    act.wait_ge(tile_done, t + 1)
                    act.wait_ge(stage_free[u], 16 * (i + 1))
                    for g in (1, 3):
                        nc.scalar.activation(stage[0:n, u, g * 512:(g + 1) * 512], acc[0:n, u, g, :],
                                             ACT.Silu).then_inc(act_out, 1)
                with act.Fori(0, NP) as i:
                    for u in range(2):
                        evacuate(2 * i + u, i, u)
                evacuate(2 * NP, NP, 0, TS)


def bias_vectors(ctx, nc, bank, rel_bias, expand, rep_p, rep_d):
    N = NC * LB + LD
    parts = [(x, min(512, N - x)) for x in range(0, N, 512)]
    sb, _, sem = region(ctx, nc)
    table = sb("table", [BUCKETS + 1, HA])
    exp_sb = sb("expand_sb", [BUCKETS + 1, N])
    vec = sb("vec", [HA, N])
    one_set, landed, product, copied, kept, repeated = (
        sem(n) for n in ("bv_one", "bv_landed", "bv_product", "bv_copied", "bv_kept", "bv_repeated"))
    vec_dram = nc.dram_tensor("bias_vec", [HA, N], F32, kind="Internal").ap()

    def vector(dve):
        nc.vector.memset(table[:], 1.0).then_inc(one_set, 1)
        for n, (x, w) in enumerate(parts):
            dve.wait_ge(product, n + 1)
            nc.vector.tensor_copy(vec[:, x:x + w], bank[0:HA, n, 0:w]).then_inc(copied, 1)

    def tensor(pe):
        pe.wait_ge(landed, 32)
        for n, (x, w) in enumerate(parts):
            pe.matmul(bank[0:HA, n, 0:w], table[:], exp_sb[:, x:x + w], start=True, stop=True).then_inc(product, 1)

    def load(sp):
        sp.dma_start(exp_sb[:], expand).then_inc(landed, 16)
        sp.wait_ge(one_set, 1)
        sp.dma_start(table[0:BUCKETS, :], rel_bias).then_inc(landed, 16)

    def repeat(sp):
        sp.wait_ge(copied, len(parts))
        sp.dma_start(vec_dram, vec[:]).then_inc(kept, 16)
        sp.wait_ge(kept, 16)
        L = NC * LB
        sp.dma_start(rep_d, bass.AP(tensor=vec_dram.tensor, offset=L, ap=[[0, NT], [N, HA], [1, LD]])
                     ).then_inc(repeated, 16)
        sp.dma_start(rep_p, bass.AP(tensor=vec_dram.tensor, offset=0, ap=[[0, P], [N, HA], [1, L]])
                     ).then_inc(repeated, 16)
    return dict(vector=vector, tensor=tensor, load=load, repeat=repeat, repeated=repeated, read=(copied, len(parts)))


def hgrn_prompt(nc, projT, projN, lbT, scan_mask, level_masks, diag_mask, ident_d, o_b, state_out, win):
    NS = HB * SEG
    with ExitStack() as ctx:
        sb, ps, sem = region(ctx, nc)
        lbp = sb("lbp", [P, 2, HB])
        lbm, lb, oml, noml = (sb(n, [P, HB]) for n in ("lbm", "lb", "oml", "noml"))
        reset = sb("reset", [P, NS])
        lmask = sb("lmask", [P, len(LEVELS), CH // 2], I32)
        dmask = sb("dmask", [P, CH], I32)
        ident = sb("ident3", [P, P])
        q, sg = sb("q", [P, 2, HB, SEG]), sb("sg", [P, 2, HB, SEG])
        v = sb("v3", [P, 2, NPR, WB])
        k, g, b, eb, qe, kh = (sb(n, [P, HB, SEG]) for n in ("k3", "g3", "b3", "eb", "qe", "kh"))
        diff, ed = sb("diff", [P, 2, NS]), sb("ed", [P, 2, NS])
        kl, ql = sb("kl", [P, 2, HB, SEG]), sb("ql", [P, 2, HB, SEG // 2])
        at = sb("at", [P, NPR, HB, CH])
        khn = sb("khn", [P, NPR, WB])
        S = sb("S", [P, 2, HB, DB])
        ost = sb("ost", [P, 2, NPR, WB])
        a_ps = ps("a_ps", [P, 2, 512])
        t_ps, o_ps, s_ps = ps("t_ps", [P, 2, 512]), ps("o_ps", [P, 2, 512]), ps("s_ps", [P, 2, 512])
        landed = [sem(f"h_landed{u}") for u in range(2)]
        ost_free = [sem(f"ost_free{u}") for u in range(2)]
        const, state_kept, mask_begun, copied = sem("h_const"), sem("state_kept"), sem("mask_begun"), sem("h_copied")
        lbs, bounds, ready = sem("h_lbs"), sem("h_bounds"), sem("h_ready")
        g_done, k_done, b_done, eb_done, qe_done = (sem(n) for n in ("g_done", "k_done", "b_done", "eb_done", "qe_done"))
        d_done, e_done, prod_done, a_done, mask_done = (sem(n) for n in ("d_done", "e_done", "prod_done", "a_done", "mask_done"))
        chain, t_done, khn_done = sem("chain"), sem("t_done"), sem("khn_done")
        ds_done, s_done, o_done, o_out = sem("ds_done"), sem("s_done"), sem("o_done"), sem("o_out")
        NL = len(LEVELS)
        ND = NL + 1
        NA = NL + 2
        NCK = 2 * NPR

        with nc.Block() as block:
            @block.sync
            def _(sp):
                for dst, src in ((lbp[:], lbT), (reset[:], scan_mask), (lmask[:], level_masks),
                                 (dmask[:], diag_mask), (ident[:], ident_d)):
                    sp.dma_start(dst, src).then_inc(const, 16)

                def load(s):
                    u, t0 = s % 2, s * SEG
                    sp.dma_start(sg[:, u], projT[12:16, :, t0:t0 + SEG].rearrange("h p t -> p h t")).then_inc(landed[u], 16)
                    sp.dma_start(q[:, u], projT[8:12, :, t0:t0 + SEG].rearrange("h p t -> p h t")).then_inc(landed[u], 16)
                    sp.dma_start(v[:, u], projN[t0:t0 + SEG, 2 * WB:3 * WB].rearrange("(c p) v -> p c v", p=P)
                                 ).then_inc(landed[u], 16)

                def store(s):
                    u, t0 = s % 2, s * SEG
                    sp.wait_ge(o_out, NPR * (s + 1) + 2)
                    sp.dma_start(o_b[t0:t0 + SEG, :].rearrange("(c p) v -> p c v", p=P), ost[:, u]).then_inc(ost_free[u], 16)

                for u in range(2):
                    sp.sem_inc(ost_free[u], 16)
                load(0)
                load(1)
                for s in range(NSEG):
                    for n in range(s, SHIFTS, NSEG):
                        shift_window(sp, win, n, copied)
                    store(s)
                    if s + 2 < NSEG:
                        sp.wait_ge(o_done, NPR * (s + 1) + 1)
                        load(s + 2)
                sp.wait_ge(s_done, NSEG * NCK + 1)
                sp.dma_start(state_out.rearrange("h k v -> k h v"), S[:, 0]).then_inc(state_kept, 16)
                sp.wait_ge(state_kept, 16)
                for u in range(2):
                    sp.wait_ge(ost_free[u], 16 * (NSEG // 2 + 1))
                sp.wait_ge(copied, 32 * SHIFTS)

            @block.scalar
            def _(act):
                act.wait_ge(lbs, 1)
                nc.scalar.activation(lbp[:], lbp[:], ACT.Exp).then_inc(lbs, 1)
                act.wait_ge(bounds, 1)
                act.sem_inc(khn_done, 2)
                with act.Fori(0, NSEG // 2) as i:
                    for u in range(2):
                        s = 2 * i + u
                        act.wait_ge(landed[u], 48 * (i + 1))
                        act.wait_ge(b_done, s + 1)
                        for h in range(HB):
                            ins = nc.scalar.activation(g[:, h], sg[:, u, h], ACT.Ln, bias=lb[:, h:h + 1], scale=oml[:, h:h + 1])
                        ins.then_inc(g_done, 1)
                        act.wait_ge(b_done, s + 2)
                        act.wait_ge(qe_done, s + 1)
                        act.wait_ge(s_done, NCK * s + 1)
                        nc.scalar.activation(eb[:], b[:], ACT.Exp).then_inc(eb_done, 1)
                        for n in range(ND):
                            act.wait_ge(d_done, ND * s + n + 1)
                            act.wait_ge(prod_done, ND * s + max(n + 1, 2))
                            h2 = LEVELS[n] if n < NL else None
                            if h2:
                                dv = diff[:, n % 2, :].rearrange("p (n two h) -> p n two h", two=2, h=h2)
                                ev = ed[:, n % 2, :].rearrange("p (n two h) -> p n two h", two=2, h=h2)
                                nc.scalar.activation(ev[:, :, 0], dv[:, :, 0], ACT.Exp, scale=-1.0)
                                nc.scalar.activation(ev[:, :, 1], dv[:, :, 1], ACT.Exp).then_inc(e_done, 1)
                            else:
                                nc.scalar.activation(ed[:, n % 2, :], diff[:, n % 2, :], ACT.Exp, scale=-1.0).then_inc(e_done, 1)
                        act.wait_ge(o_done, NPR * s + 1)
                        for c in range(NPR):
                            act.wait_ge(t_done, NPR * s + c + 1)
                            nc.scalar.activation(khn[:, c], t_ps[:, c % 2], ACT.Copy).then_inc(khn_done, 1)
                        act.wait_ge(ost_free[u], 16 * (i + 1))
                        for c in range(NPR):
                            act.wait_ge(o_done, NPR * s + c + 2)
                            nc.scalar.activation(ost[:, u, c], o_ps[:, c % 2], ACT.Copy).then_inc(o_out, 1)

            @block.gpsimd
            def _(pool):
                nc.gpsimd.memset(kl[:], 0.0).then_inc(ready, 1)
                with pool.Fori(0, NSEG) as s:
                    pool.wait_ge(b_done, s + 2)
                    for n in range(ND):
                        pool.wait_ge(e_done, ND * s + max(n + 1, 2))
                        m = LEVELS[n] if n < NL else CH // 2
                        mid = m - 1 if n < NL else CH - 1
                        bv = b[:].rearrange("p h (n w) -> p (h n) w", w=2 * m)
                        dv = diff[:, n % 2, :].rearrange("p (n w) -> p n w", w=2 * m)
                        nc.gpsimd.tensor_tensor(dv, bv, bv[:, :, mid:mid + 1].to_broadcast([P, NS // (2 * m), 2 * m]),
                                                ALU.subtract).then_inc(d_done, 1)

            @block.vector
            def _(dve):
                dve.wait_ge(const, 16 * 5)
                steps = [0]

                def then(ins):
                    steps[0] += 1
                    ins.then_inc(chain, 1)
                    dve.wait_ge(chain, steps[0])

                then(nc.vector.tensor_tensor(lbm[:], lbp[:, 0], lbp[:, 1], ALU.max))
                for r in range(2):
                    ins = nc.vector.tensor_tensor(lbp[:, r], lbp[:, r], lbm[:], ALU.subtract)
                    if r == 0:
                        then(ins)
                ins.then_inc(lbs, 1)
                dve.wait_ge(lbs, 2)
                then(nc.vector.tensor_tensor(lbm[:], lbp[:, 0], lbp[:, 1], ALU.add))
                then(nc.vector.reciprocal(lbm[:], lbm[:]))
                then(nc.vector.tensor_tensor(lb[:], lbp[:, 0], lbm[:], ALU.mult))
                then(nc.vector.tensor_scalar(oml[:], lb[:], -1.0, 1.0, ALU.mult, ALU.add))
                nc.vector.tensor_scalar(noml[:], oml[:], -1.0, None, ALU.mult).then_inc(bounds, 1)
                dve.wait_ge(bounds, 1)
                nc.vector.memset(at[:], 0.0)
                nc.vector.memset(S[:, 0], 0.0).then_inc(s_done, 1)
                dve.wait_ge(s_done, 1)
                dve.wait_ge(ready, 1)
                dve.sem_inc(e_done, 2)
                dve.sem_inc(prod_done, 2)
                dve.sem_inc(mask_done, 2)
                dve.sem_inc(qe_done, 1)
                dve.sem_inc(o_done, 1)
                dve.sem_inc(o_out, 2)
                dve.sem_inc(b_done, 1)

                def mask_step(s, n):
                    dve.wait_ge(mask_done, NA * s + n + 2)
                    dve.wait_ge(a_done, NA * s + n + 1)
                    dve.sem_inc(mask_begun, 1)
                    if n < NL:
                        h2 = LEVELS[n]
                        nb = CH // (2 * h2)
                        dst = at[:].rearrange("p c h (n two j) -> p (c h) n two j", two=2, j=h2)[:, :, :, 1, :]
                        src = a_ps[:, n % 2, :].rearrange("p (a n j) -> p a n j", n=nb, j=h2)
                        m = lmask[:, n, :].rearrange("p (n j) -> p n j", j=h2).unsqueeze(1).to_broadcast(
                            [P, NPR * HB, nb, h2])
                    else:
                        x = n - NL
                        dst = at[:, 2 * x:2 * x + 2].rearrange("p c h t -> p (c h) t")
                        src = a_ps[:, n % 2, :].rearrange("p (a t) -> p a t", t=CH)
                        m = dmask[:].unsqueeze(1).to_broadcast([P, 2 * HB, CH])
                    nc.vector.copy_predicated(dst, m, src).then_inc(mask_done, 1)

                with dve.Fori(0, NSEG // 2) as i:
                    for u in range(2):
                        s = 2 * i + u
                        dve.wait_ge(landed[u], 48 * (i + 1))
                        for h in range(HB):
                            ins = nc.vector.tensor_scalar(k[:, h], sg[:, u, h], noml[:, h:h + 1], oml[:, h:h + 1],
                                                          ALU.mult, ALU.add)
                        ins.then_inc(k_done, 1)
                        dve.wait_ge(g_done, s + 1)
                        nc.vector.tensor_tensor_scan(b[:].rearrange("p h t -> p (h t)"), reset[:],
                                                     g[:].rearrange("p h t -> p (h t)"), 0.0,
                                                     ALU.mult, ALU.add).then_inc(b_done, 1)
                        dve.wait_ge(k_done, s + 1)
                        for n in range(ND):
                            dve.wait_ge(e_done, ND * s + n + 3)
                            e = ed[:, n % 2, :]
                            if n < NL:
                                h2 = LEVELS[n]
                                dve.wait_ge(a_done, NA * s + n - 1) if n >= 2 else dve.wait_ge(o_done, NPR * s + 1)
                                cut = lambda ap: ap.rearrange("p (n two j) -> p n two j", two=2, j=h2)
                                kv = cut(k[:].rearrange("p h t -> p (h t)"))
                                qv = cut(q[:, u].rearrange("p h t -> p (h t)"))
                                klv = cut(kl[:, n % 2].rearrange("p h t -> p (h t)"))
                                qlv = ql[:, n % 2].rearrange("p h t -> p (h t)").rearrange("p (n j) -> p n j", j=h2)
                                nc.vector.tensor_tensor(klv[:, :, 0], kv[:, :, 0], cut(e)[:, :, 0], ALU.mult)
                                nc.vector.tensor_tensor(qlv, qv[:, :, 1], cut(e)[:, :, 1], ALU.mult).then_inc(prod_done, 1)
                                if n:
                                    mask_step(s, n - 1)
                            else:
                                nc.vector.tensor_tensor(kh[:].rearrange("p h t -> p (h t)"), k[:].rearrange("p h t -> p (h t)"),
                                                        e, ALU.mult).then_inc(prod_done, 1)
                        dve.wait_ge(eb_done, s + 1)
                        nc.vector.tensor_tensor(qe[:], q[:, u], eb[:], ALU.mult).then_inc(qe_done, 1)
                        for n in range(NL - 1, NA):
                            mask_step(s, n)
                        for c in range(NCK):
                            dve.wait_ge(ds_done, NCK * s + c + 1)
                            dve.wait_ge(s_done, NCK * s + c + 1)
                            for h in range(HB):
                                ins = nc.vector.scalar_tensor_tensor(
                                    S[:, (c + 1) % 2, h], S[:, c % 2, h], eb[:, h, (c + 1) * CH - 1:(c + 1) * CH],
                                    s_ps[:, c % 2, h * DB:(h + 1) * DB], ALU.mult, ALU.add)
                            ins.then_inc(s_done, 1)

            @block.tensor
            def _(pe):
                with pe.Fori(0, NSEG // 2) as i:
                    for u in range(2):
                        s = 2 * i + u

                        def a_step(n):
                            pe.wait_ge(mask_done, NA * s + n + 1)
                            if n < NL:
                                pe.wait_ge(prod_done, ND * s + n + 3)
                                todo = [(c, x, h) for c in range(NPR) for x in range(2) for h in range(HB)]
                            else:
                                pe.wait_ge(k_done, s + 1)
                                todo = [(c, x, h) for c in (2 * (n - NL), 2 * (n - NL) + 1) for x in range(2) for h in range(HB)]
                            for c, x, h in todo:
                                t0 = (2 * c + x) * CH
                                if n < NL:
                                    lhs, rhs = kl[:, n % 2, h, t0:t0 + CH], ql[:, n % 2, h, t0 // 2:(t0 + CH) // 2]
                                    col, w = (c * HB + h) * CH // 2, CH // 2
                                else:
                                    lhs, rhs = k[:, h, t0:t0 + CH], q[:, u, h, t0:t0 + CH]
                                    col, w = ((c % 2) * HB + h) * CH, CH
                                mm = pe.matmul(a_ps[x * CH:(x + 1) * CH, n % 2, col:col + w], lhs, rhs, start=True, stop=True)
                            mm.then_inc(a_done, 1)

                        pe.wait_ge(landed[u], 48 * (i + 1))
                        for n in range(NA):
                            a_step(n)
                        pe.wait_ge(prod_done, ND * s + ND + 2)
                        for c in range(NPR):
                            pe.wait_ge(khn_done, NPR * s + c + 1)
                            for h in range(HB):
                                mm = pe.transpose(t_ps[:, c % 2, h * P:(h + 1) * P], kh[:, h, c * P:(c + 1) * P], ident[:])
                            mm.then_inc(t_done, 1)
                        pe.wait_ge(qe_done, s + 2)
                        pe.wait_ge(mask_done, NA * s + NA + 2)
                        for c in range(NCK):
                            r = slice((c % 2) * CH, (c % 2 + 1) * CH)
                            pr = c // 2
                            pe.wait_ge(khn_done, NPR * s + pr + 3)
                            pe.wait_ge(s_done, NCK * s + max(c, 1))
                            for h in range(HB):
                                mm = pe.matmul(s_ps[:, c % 2, h * DB:(h + 1) * DB], khn[r, pr, h * DB:(h + 1) * DB],
                                               v[r, u, pr, h * DB:(h + 1) * DB], start=True, stop=True)
                            mm.then_inc(ds_done, 1)
                            pe.wait_ge(s_done, NCK * s + c + 1)
                            if c % 2 == 0:
                                pe.wait_ge(o_out, NPR * s + pr + 1)
                            for h in range(HB):
                                o = o_ps[r, pr % 2, h * DB:(h + 1) * DB]
                                pe.matmul(o, qe[:, h, c * CH:(c + 1) * CH], S[:, c % 2, h], start=True, stop=False)
                                mm = pe.matmul(o, at[r, pr, h], v[r, u, pr, h * DB:(h + 1) * DB], start=False, stop=True)
                            if c % 2:
                                mm.then_inc(o_done, 1)


def hgrn_sample(ctx, nc, bank, bank_read, projT, projN, lbT, scan_mask, level_masks, row_mask, ident_d, state_in, o_b, state_out):
    N = HB * TS
    levels = [h for h in LEVELS if h < NT]
    NL = len(levels)
    flat = lambda ap: ap.rearrange("p h t -> p (h t)")
    sb, _, sem = region(ctx, nc)
    lbp, lbs_ = sb("s_lbp", [P, 2, HB]), sb("s_lbs", [P, 4, HB])
    reset, masks = sb("s_reset", [P, N]), sb("s_masks", [TS, NL + 1, TS], I32)
    rowm, ident = sb("s_rowm", [TS, NB]), sb("s_ident", [P, P])
    q, sg, v = sb("s_q", [P, HB, TS]), sb("s_sg", [P, HB, TS]), sb("s_v", [TS, WB])
    S0 = sb("s_S0", [P, NB, HB, DB])
    k, g, b, eb, qe, kh, diff, ed = (sb(f"s_{n}", [P, HB, TS]) for n in ("k", "g", "b", "eb", "qe", "kh", "diff", "ed"))
    kl, ql = sb("s_kl", [P, HB, TS]), sb("s_ql", [P, HB, TS])
    at, khn, khm = sb("s_at", [TS, HB, TS]), sb("s_khn", [TS, WB]), sb("s_khm", [TS, NB, WB])
    qem, ost = sb("s_qem", [P, NB, HB, TS]), sb("s_ost", [TS, WB])
    a_ps = bank[0:TS, 0, 0:HB * TS].rearrange("p (h t) -> p h t", h=HB)
    t_ps, o_ps, s_ps = bank[0:TS, 1], bank[0:TS, 2], bank[:, 3:5]
    landed, stored, chain, act_done, a_done, took = (sem(f"s_{n}") for n in ("landed", "stored", "chain", "act_done", "a_done", "took"))
    t_done, khm_done, ds_done, s_done, o_done, mems = (sem(f"s_{n}") for n in ("t_done", "khm_done", "ds_done", "s_done", "o_done", "mems"))
    lvl = sem("s_lvl")
    def sync(sp):
        for dst, src in ((lbp[:], lbT), (reset[:], scan_mask), (masks[:], level_masks), (rowm[:], row_mask),
                         (ident[:], ident_d), (q[:], projT[8:12, :, T:TT].rearrange("h p t -> p h t")),
                         (sg[:], projT[12:16, :, T:TT].rearrange("h p t -> p h t")),
                         (v[:], projN[T:TT, 2 * WB:3 * WB]),
                         (S0[:], state_in.rearrange("b h k v -> k b h v"))):
            sp.dma_start(dst, src).then_inc(landed, 16)

    def store(sp):
        sp.wait_ge(s_done, NB)
        sp.dma_start(state_out.rearrange("b h k v -> k b h v"), S0[:]).then_inc(stored, 16)
        sp.wait_ge(took, 4 + 1)
        sp.dma_start(o_b[T:TT, :], ost[:]).then_inc(stored, 16)
        sp.wait_ge(stored, 32)

    def gpsimd(pool):
        nc.gpsimd.memset(qem[:], 0.0).then_inc(mems, 1)
        nc.gpsimd.memset(at[:], 0.0).then_inc(mems, 1)

    def scalar(act):
        act.wait_ge(lvl, 1)
        nc.scalar.activation(lbp[:], lbp[:], ACT.Exp).then_inc(act_done, 1)
        act.wait_ge(lvl, 2)
        for h in range(HB):
            ins = nc.scalar.activation(g[:, h], sg[:, h], ACT.Ln, bias=lbs_[:, 1, h:h + 1], scale=lbs_[:, 2, h:h + 1])
        ins.then_inc(act_done, 1)
        act.wait_ge(lvl, 3)
        nc.scalar.activation(eb[:], b[:], ACT.Exp).then_inc(act_done, 1)
        for n in range(NL + 1):
            act.wait_ge(lvl, 4 + n)
            if n < NL:
                cut = lambda ap: flat(ap).rearrange("p (n two j) -> p n two j", two=2, j=levels[n])
                nc.scalar.activation(cut(ed[:])[:, :, 0], cut(diff[:])[:, :, 0], ACT.Exp, scale=-1.0)
                nc.scalar.activation(cut(ed[:])[:, :, 1], cut(diff[:])[:, :, 1], ACT.Exp).then_inc(act_done, 1)
            else:
                nc.scalar.activation(ed[:], diff[:], ACT.Exp, scale=-1.0).then_inc(act_done, 1)

    def vector(dve):
        steps = [0]

        def then(ins, more=None):
            steps[0] += 1
            ins.then_inc(chain, 1)
            dve.wait_ge(chain, steps[0])
            if more is not None:
                dve.sem_inc(more, 1)

        tt = nc.vector.tensor_tensor
        dve.wait_ge(landed, 16 * 9)
        then(tt(lbs_[:, 0], lbp[:, 0], lbp[:, 1], ALU.max))
        then(tt(lbp[:, 0], lbp[:, 0], lbs_[:, 0], ALU.subtract))
        then(tt(lbp[:, 1], lbp[:, 1], lbs_[:, 0], ALU.subtract), lvl)
        dve.wait_ge(act_done, 1)
        then(tt(lbs_[:, 0], lbp[:, 0], lbp[:, 1], ALU.add))
        then(nc.vector.reciprocal(lbs_[:, 0], lbs_[:, 0]))
        then(tt(lbs_[:, 1], lbp[:, 0], lbs_[:, 0], ALU.mult))
        then(nc.vector.tensor_scalar(lbs_[:, 2], lbs_[:, 1], -1.0, 1.0, ALU.mult, ALU.add))
        then(nc.vector.tensor_scalar(lbs_[:, 3], lbs_[:, 2], -1.0, None, ALU.mult), lvl)
        for h in range(HB):
            then(nc.vector.tensor_scalar(k[:, h], sg[:, h], lbs_[:, 3, h:h + 1], lbs_[:, 2, h:h + 1], ALU.mult, ALU.add))
        dve.wait_ge(act_done, 2)
        then(nc.vector.tensor_tensor_scan(flat(b[:]), reset[:], flat(g[:]), 0.0, ALU.mult, ALU.add), lvl)
        dve.wait_ge(mems, 2)
        for n in range(NL + 1):
            w, mid = (2 * levels[n], levels[n] - 1) if n < NL else (NT, NT - 1)
            bv = flat(b[:]).rearrange("p (n w) -> p n w", w=w)
            then(tt(flat(diff[:]).rearrange("p (n w) -> p n w", w=w), bv,
                    bv[:, :, mid:mid + 1].to_broadcast([P, N // w, w]), ALU.subtract), lvl)
            dve.wait_ge(act_done, 4 + n)
            if n == NL:
                break
            then(tt(kl[:], k[:], ed[:], ALU.mult))
            then(tt(ql[:], q[:], ed[:], ALU.mult), took)
            dve.wait_ge(a_done, n + 1)
            then(nc.vector.copy_predicated(at[:], masks[:, n].unsqueeze(1).to_broadcast([TS, HB, TS]), a_ps))
        then(tt(kh[:], k[:], ed[:], ALU.mult), took)
        dve.wait_ge(a_done, NL + 1)
        then(nc.vector.copy_predicated(at[:], masks[:, NL].unsqueeze(1).to_broadcast([TS, HB, TS]), a_ps))
        then(tt(qe[:], q[:], eb[:], ALU.mult))
        for s in range(NB):
            c = slice(s * NT, (s + 1) * NT)
            ins = nc.vector.tensor_copy(qem[:, s, :, c], qe[:, :, c])
        ins.then_inc(khm_done, 1)
        dve.wait_ge(t_done, 1)
        then(nc.vector.tensor_copy(khn[:], t_ps))
        for s in range(NB):
            ins = nc.vector.tensor_scalar(khm[:, s], khn[:], rowm[:, s:s + 1], None, ALU.mult)
        ins.then_inc(khm_done, 1)
        dve.wait_ge(o_done, 1)
        then(nc.vector.tensor_copy(ost[:], o_ps), took)
        for s in range(NB):
            dve.wait_ge(ds_done, s + 1)
            for h in range(HB):
                e = s * NT + NT - 1
                ins = nc.vector.scalar_tensor_tensor(S0[:, s, h], S0[:, s, h], eb[:, h, e:e + 1],
                                                     s_ps[:, s % 2, h * DB:(h + 1) * DB], ALU.mult, ALU.add)
            ins.then_inc(s_done, 1)

    def tensor(pe):
        pe.wait_ge(*bank_read)
        for n in range(NL + 1):
            pe.wait_ge(took, n + 1)
            lhs, rhs = (kl, ql) if n < NL else (k, q)
            for h in range(HB):
                mm = pe.matmul(a_ps[:, h], lhs[:, h], rhs[:, h], start=True, stop=True)
            mm.then_inc(a_done, 1)
        for h in range(HB):
            mm = pe.transpose(t_ps[:, h * P:(h + 1) * P], kh[:, h], ident[:])
        mm.then_inc(t_done, 1)
        pe.wait_ge(khm_done, 1)
        for h in range(HB):
            o = o_ps[:, h * DB:(h + 1) * DB]
            for s in range(NB):
                pe.matmul(o, qem[:, s, h], S0[:, s, h], start=(s == 0), stop=False)
            mm = pe.matmul(o, at[:, h], v[:, h * DB:(h + 1) * DB], start=False, stop=True)
        mm.then_inc(o_done, 1)
        pe.wait_ge(khm_done, 2)
        for s in range(NB):
            if s >= 2:
                pe.wait_ge(s_done, s - 1)
            for h in range(HB):
                mm = pe.matmul(s_ps[:, s % 2, h * DB:(h + 1) * DB], khm[:, s, h * DB:(h + 1) * DB],
                               v[:, h * DB:(h + 1) * DB], start=True, stop=True)
            mm.then_inc(ds_done, 1)
    return dict(load=sync, store=store, gpsimd=gpsimd, scalar=scalar, vector=vector, tensor=tensor, read=(s_done, NB))


def attention_prompt(nc, projT, projN, rep_p, ident_d, partials, win):
    NBK = T // P
    units = []
    for c in range(NC):
        for x in range(2):
            for b in range(0, NBK, 2):
                units.append((c, x, b))
    NU = len(units)
    NGRP = NU // 4
    WARM = 14

    def block_keys(c, b):
        d = DILS[c]
        nj = NBK // d
        r, j = b // nj, b % nj
        q0 = r + d * P * j
        return (q0, q0 - d * P, 2) if j else (q0, q0, 1)

    def tiles(c, b0):
        out = []
        for y in range(2):
            n = block_keys(c, b0 + y)[2]
            out += [(y, b0 + y - n + 1 + m, 2 - n + m) for m in range(n)]
        return out

    def unit(n):
        return (n // NU, *units[n % NU])

    with ExitStack() as ctx:
        sb, ps, sem = region(ctx, nc)
        ident = sb("a_ident", [P, P])
        raw = sb("a_raw", [P, 2, T])
        q2, khi, klo = (sb(f"a_{n}", [P, 2, 2, T], F32R) for n in ("q2", "khi", "klo"))
        v = sb("a_v", [P, 2, NC, NBK, P])
        bias = sb("a_bias", [P, 2, 2, NC, 2 * P])
        prob = sb("a_prob", [P, 4, 2, 2 * P])
        probT = sb("a_probT", [P, 3, 4, P])
        stage = sb("a_stage", [P, 2, NBK, 2, OW])
        s_ps, t_ps, o_ps = ps("a_s_ps", [P, 3, 512]), ps("a_t_ps", [P, 3, 512]), ps("a_o_ps", [P, 2, 512])
        landed = [sem(f"a_landed{u}") for u in range(2)]
        stage_free = [sem(f"a_stage_free{w}") for w in range(2)]
        const, s_done, p_done, p_turn, e_done = (sem(f"a_{n}") for n in ("const", "s_done", "p_done", "p_turn", "e_done"))
        t_done, pt_done, pv_done, o_out = (sem(f"a_{n}") for n in ("t_done", "pt_done", "pv_done", "o_out"))
        raw_landed = [sem(f"a_raw_landed{w}") for w in range(2)]
        copied = sem("a_copied")
        hi_done, lo_done, split_turn = sem("a_hi_done"), sem("a_lo_done"), sem("a_split_turn")
        bias_landed = [sem(f"a_bias_landed{u}") for u in range(2)]
        NLD = 6

        with nc.Block() as block:
            @block.sync
            def _(sp):
                sp.dma_start(ident[:], ident_d).then_inc(const, 16)
                sp.sem_inc(stage_free[0], 16)
                sp.sem_inc(stage_free[1], 16)

                def load_bias(g):
                    u = g % 2
                    L = HA * NC * LB
                    for x in range(2):
                        src = bass.AP(tensor=rep_p.tensor, offset=(2 * g + x) * NC * LB + P - 1,
                                      ap=[[L - 1, P], [LB, NC], [1, 2 * P]])
                        sp.dma_start(bias[:, u, x], src).then_inc(bias_landed[u], 16)

                def load_values(g):
                    u = g % 2
                    for c, d in enumerate(DILS):
                        rows = projN[0:T, g * P:(g + 1) * P].rearrange("(j p r) d -> p r j d", p=P, r=d)
                        dst = v[:, u, c].rearrange("p (r j) d -> p r j d", r=d)
                        if c == 1:
                            for j in range(NBK // d):
                                sp.dma_start(dst[:, :, j], rows[:, :, j]).then_inc(landed[u], 16)
                        else:
                            sp.dma_start(dst[:, 0] if d == 1 else dst[:, :, 0], rows[:, 0] if d == 1 else rows[:, :, 0]
                                         ).then_inc(landed[u], 16)

                load_bias(0)
                for w in range(2):
                    sp.wait_ge(raw_landed[w], 32)
                load_values(0)
                load_bias(1)
                load_values(1)
                for g in range(NG):
                    for c, d in enumerate(DILS):
                        w = (NC * g + c) % 2
                        sp.wait_ge(o_out, NGRP * g + NGRP // NC * (c + 1) + 2)
                        rows = partials[c, :, 2 * g:2 * g + 2, :].rearrange("(j p r) h w -> p r j (h w)", p=P, r=d)
                        src = stage[:, w].rearrange("p (r j) h w -> p r j (h w)", r=d)
                        if c == 1:
                            for j in range(NBK // d):
                                sp.dma_start(rows[:, :, j], src[:, :, j]).then_inc(stage_free[w], 16)
                        else:
                            a, b = (rows[:, 0], src[:, 0]) if d == 1 else (rows[:, :, 0], src[:, :, 0])
                            for half in range(4):
                                m = NBK // 4
                                sp.dma_start(a[:, half * m:(half + 1) * m], b[:, half * m:(half + 1) * m]
                                             ).then_inc(stage_free[w], 16)
                        if SHIFTS + NC * g + c < 2 * NB:
                            shift_window(sp, win, SHIFTS + NC * g + c, copied)
                    if g + 2 < NG:
                        sp.wait_ge(pv_done, NU * (g + 1) + 3)
                        load_bias(g + 2)
                        load_values(g + 2)
                for w in range(2):
                    sp.wait_ge(stage_free[w], 16 + 64 * NC * NG // 2)
                sp.wait_ge(copied, 32 * (2 * NB - SHIFTS))

            @block.gpsimd
            def _(pool):
                def load(g, x, w):
                    for half in range(2):
                        pool.dma_start(raw[half * DA:(half + 1) * DA, w], projT[w * NG + g, x * DA:(x + 1) * DA, 0:T]
                                       ).then_inc(raw_landed[w], 16)

                with pool.Fori(0, NG // 2) as i:
                    for u in range(2):
                        g = 2 * i + u
                        load(g, 0, 0)
                        for x in range(2):
                            for w in range(2):
                                item = 4 * g + 2 * x + w
                                if (x, w) != (1, 1):
                                    load(g, x + w, 1 - w)
                                pool.wait_ge(raw_landed[w], 32 * (2 * g + x + 1))
                                if x == 0 and w == 0:
                                    pool.wait_ge(s_done, NU * (g + 1))
                                pool.sem_inc(split_turn, 1)
                                hi = (q2 if w == 0 else khi)[:, u, x]
                                nc.gpsimd.tensor_copy(hi, raw[:, w]).then_inc(hi_done, 1)
                                pool.wait_ge(hi_done, item + 1)
                                if w == 0:
                                    r = slice(DA, P)
                                    nc.gpsimd.tensor_tensor(q2[r, u, x], raw[r, w], q2[r, u, x].bitcast(F32),
                                                            ALU.subtract).then_inc(lo_done, 1)
                                else:
                                    nc.gpsimd.tensor_tensor(klo[:, u, x], raw[:, w], khi[:, u, x].bitcast(F32),
                                                            ALU.subtract).then_inc(lo_done, 1)
                                pool.wait_ge(lo_done, item + 1)

            def stage_slot(u, c):
                return (NC * u + c) % 2

            @block.vector
            def _(dve):
                dve.sem_inc(p_done, 3)
                dve.sem_inc(pt_done, 3)
                dve.sem_inc(o_out, 2)
                with dve.Fori(0, NG // 2) as i:
                    for n in range(2 * NU + 3):
                        if n < 2 * NU:
                            u, c, x, b = unit(n)
                            w = stage_slot(u, c)
                            if n % NU == 0:
                                dve.wait_ge(bias_landed[u], 32 * (i + 1))
                            if n % (NU // NC) == 0:
                                k = len([1 for m in range(NC * u + c) if m % 2 == w])
                                dve.wait_ge(stage_free[w], 16 + 64 * (NC * i + k))
                            dve.wait_ge(t_done, 2 * NU * i + n + 1)
                            dve.wait_ge(s_done, 2 * NU * (i + 1) + n + 1)
                            dve.sem_inc(p_turn, 1)
                            for y in range(2):
                                m = P * block_keys(c, b + y)[2]
                                ins = nc.vector.tensor_tensor_reduce(
                                    prob[:, n % 4, y, 2 * P - m:], s_ps[:, n % 3, y * 2 * P + 2 * P - m:(y + 1) * 2 * P],
                                    bias[:, u, x, c, 2 * P - m:], -SCALE, 3e38, ALU.add, ALU.min,
                                    stage[:, w, b + y, x, DA + 1:DA + 2])
                            ins.then_inc(p_done, 1)
                        if n >= 3:
                            m = n - 3
                            _, c, _, b = unit(m)
                            width = P * len(tiles(c, b))
                            dve.wait_ge(pv_done, 2 * NU * i + m + 1)
                            dve.wait_ge(t_done, 2 * NU * i + m + 5)
                            nc.vector.tensor_copy(probT[:, m % 3].rearrange("p a k -> p (a k)")[:, 0:width],
                                                  t_ps[:, m % 3, 0:width]).then_inc(pt_done, 1)

            @block.scalar
            def _(act):
                with act.Fori(0, NG // 2) as i:
                    for n in range(2 * NU + 5):
                        if n < 2 * NU:
                            u, c, x, b = unit(n)
                            act.wait_ge(p_done, 2 * NU * i + n + 4)
                            for y in range(2):
                                m = P * block_keys(c, b + y)[2]
                                pr = prob[:, n % 4, y, 2 * P - m:]
                                st = stage[:, stage_slot(u, c), b + y, x]
                                ins = nc.scalar.activation(pr, pr, ACT.Exp, bias=st[:, DA + 1:DA + 2], scale=-1.0,
                                                           accum_out=st[:, DA:DA + 1])
                            ins.then_inc(e_done, 1)
                        m = n - 5
                        if m >= 0 and m % 4 == 3:
                            u, c, x, b = unit(m - 3)
                            act.wait_ge(pv_done, 2 * NU * i + m + 4)
                            nc.scalar.activation(stage[:, stage_slot(u, c), b:b + 8, x, 0:DA],
                                                 o_ps[:, (m // 4) % 2].rearrange("p (b d) -> p b d", d=DA),
                                                 ACT.Copy).then_inc(o_out, 1)

            @block.tensor
            def _(pe):
                def warm_up():
                    for _ in range(WARM):
                        pe.matmul(t_ps[:, 0, 0:P], ident[:], ident[:], start=True, stop=True)

                pe.wait_ge(const, 16)
                pe.sem_inc(t_done, 4)
                pe.sem_inc(pv_done, 3)
                pe.sem_inc(s_done, 2 * NU)
                with pe.Fori(0, NG // 2) as i:
                    pe.wait_ge(pt_done, 2 * NU * i + 3)
                    pe.wait_ge(hi_done, 8 * i + 1)
                    warm_up()
                    for n in range(2 * NU + 4):
                        if n < 2 * NU:
                            u, c, x, b = unit(n)
                            d = DILS[c]
                            if c == 0 and b == 0:
                                pe.wait_ge(lo_done, 8 * i + 4 * u + 2 * x + 2)
                            pe.wait_ge(p_done, 2 * NU * i + n + 1)
                            for y in range(2):
                                q0, k0, m = block_keys(c, b + y)
                                ks = slice(k0, k0 + d * (m * P - 1) + 1, d)
                                for a, k2 in enumerate((khi, klo)):
                                    mm = pe.matmul(s_ps[:, n % 3, y * 2 * P + (2 - m) * P:(y + 1) * 2 * P],
                                                   q2[:, u, x, q0:q0 + d * (P - 1) + 1:d], k2[:, u, x, ks],
                                                   start=(a == 0), stop=(a == 1))
                            mm.then_inc(s_done, 1)
                        if 2 <= n < 2 * NU + 2:
                            m = n - 2
                            _, c, x, b = unit(m)
                            pe.wait_ge(e_done, 2 * NU * i + m + 1)
                            pe.wait_ge(pt_done, 2 * NU * i + m + 1)
                            for a, (y, _, place) in enumerate(tiles(c, b)):
                                mm = pe.transpose(t_ps[:, m % 3, a * P:(a + 1) * P],
                                                  prob[:, m % 4, y, place * P:(place + 1) * P], ident[:])
                            mm.then_inc(t_done, 1)
                        if n >= 4:
                            m = n - 4
                            u, c, x, b = unit(m)
                            if m % NU == 0:
                                pe.wait_ge(landed[u], 16 * NLD * (i + 1))
                            pe.wait_ge(pt_done, 2 * NU * i + m + 4)
                            if m % 4 == 0:
                                pe.wait_ge(o_out, 2 * NGRP * i + m // 4 + 1)
                            ts = tiles(c, b)
                            for a, (y, vt, _) in enumerate(ts):
                                col = (2 * (m % 4) + y) * DA
                                mm = pe.matmul(o_ps[:, (m // 4) % 2, col:col + DA], probT[:, m % 3, a],
                                               v[:, u, c, vt, x * DA:(x + 1) * DA],
                                               start=(a == 0 or ts[a - 1][0] != y),
                                               stop=(a == len(ts) - 1 or ts[a + 1][0] != y))
                            mm.then_inc(pv_done, 1)


def attention_sample(ctx, nc, bank, bank_read, repeated, projT, projN, cache_kT, cache_v, rep_d, ident_d, attn_s):
    FAR = WIN - 512
    NL = WROWS * NT
    NH = (WIN - FAR) // 2
    NK = NL + NH + NT
    R = HA * NT
    ktiles = ([slice(a, NL, NT) for a in range(NT)] + [slice(NL + a * P, NL + (a + 1) * P) for a in range(NH // P)]
              + [slice(NL + NH, NK)])
    rows_of = [P] * (NT + NH // P) + [NT]
    NKT = len(ktiles)
    NVL = 2 + NH // P
    sb, _, sem = region(ctx, nc)
    ident = sb("d_ident", [P, P])
    klow, khigh = sb("d_klow", [P, 2, NG, NL]), sb("d_khigh", [P, 2, NG, NH])
    vlow, vhigh = sb("d_vlow", [P, 2, NT, WA]), sb("d_vhigh", [P, 2, NH // P, WA])
    vn = sb("d_vn", [NT, 2, WA])
    qs, ks = sb("d_qs", [P, NG, TS]), sb("d_ks", [P, NG, TS])
    qb = sb("d_qb", [P, NG, 2, R])
    kn = sb("d_kn", [P, 2, NG, NT])
    bias = sb("d_bias", [R, WIN + NT])
    prob, probT = sb("d_prob", [R, 2, NK]), sb("d_probT", [P, 2, NKT, R])
    mn, nm, den = sb("d_mn", [R, 4]), sb("d_nm", [R, 2]), sb("d_den", [R, 2])
    out = sb("d_out", [R, 2, WA])
    s_ps, t_ps, o_ps = bank[0:R, 0:3], bank[:, 3:5], bank[0:R, 5:7]
    k_landed, v_landed, out_free = ([sem(f"d_{n}{u}") for u in range(2)] for n in ("k_landed", "v_landed", "out_free"))
    const, bias_landed, zeroed, q_done, qk_done, turn, min_done, nm_done = (
        sem(f"d_{n}") for n in ("const", "bias_landed", "zeroed", "q_done", "qk_done", "turn", "min_done", "nm_done"))
    e_done, r_done, t_done, pt_done, pv_done, o_done, turn_pe = (
        sem(f"d_{n}") for n in ("e_done", "r_done", "t_done", "pt_done", "pv_done", "o_done", "turn_pe"))

    def turns(eng, turn):
        with eng.Fori(0, NB // 2 - 1) as i:
            for u in range(2):
                turn(2 * i + u, i, u, 2)
        for u in range(2):
            turn(NB - 2 + u, NB // 2 - 1, u, 1 - u)

    def load_keys(sp, s):
        u, src = s % 2, cache_kT[s].rearrange("(g p) a m r -> p g a (m r)", p=P)
        sp.dma_start(klow[:, u], src[:, :, 0]).then_inc(k_landed[u], 16)
        sp.dma_start(khigh[:, u], src[:, :, 1, NL - NH:NL]).then_inc(k_landed[u], 16)

    def load_values(sp, s):
        u, src = s % 2, cache_v[s].rearrange("(m a r) d -> m a r d", a=2, r=NT)
        sp.dma_start(vlow[:, u], src[:, 0]).then_inc(v_landed[u], 16)
        for a in range(NH // P):
            m0 = FAR // (2 * NT) + a * P // NT
            sp.dma_start(vhigh[:, u, a], src[m0:m0 + P // NT, 1]).then_inc(v_landed[u], 16)
        sp.dma_start(vn[:, u], projN[T + s * NT:T + (s + 1) * NT, 0:WA]).then_inc(v_landed[u], 16)

    def load(sp):
        sp.dma_start(ident[:], ident_d).then_inc(const, 16)
        sp.dma_start(qs[:], projT[0:NG, :, T:TT].rearrange("g p t -> p g t")).then_inc(const, 16)
        sp.dma_start(ks[:], projT[NG:2 * NG, :, T:TT].rearrange("g p t -> p g t")).then_inc(const, 16)
        for s in range(2):
            load_keys(sp, s)
        for s in range(2):
            load_values(sp, s)

    def sync(sp):
        for s in range(NB):
            if s + 2 < NB:
                sp.wait_ge(qk_done, s + 1)
                load_keys(sp, s + 2)
                sp.wait_ge(pv_done, s + 3)
                load_values(sp, s + 2)
            sp.wait_ge(o_done, s + 3)
            for h in range(HA):
                sp.dma_start(attn_s[s * NT:(s + 1) * NT, h * DA:(h + 1) * DA],
                             out[h * NT:(h + 1) * NT, s % 2, h * DA:(h + 1) * DA]).then_inc(out_free[s % 2], 16)
        for u in range(2):
            sp.wait_ge(out_free[u], 16 * HA * (NB // 2 + 1))

    def gpsimd(pool):
        nc.gpsimd.memset(qb[:], 0.0).then_inc(zeroed, 1)

    def vector(dve):
        def queries(s, u):
            c = bass.ds(s * NT, NT)
            for x in range(2):
                r = slice(x * DA, (x + 1) * DA)
                for g in range(NG):
                    col = (2 * g + x) * NT
                    nc.vector.tensor_copy(qb[r, g, u, col:col + NT], qs[r, g, c])
            nc.vector.tensor_copy(kn[:, u], ks[:, :, c]).then_inc(q_done, 1)

        def scores(s, u):
            dve.wait_ge(t_done, s + 1)
            dve.wait_ge(qk_done, s + 1)
            dve.sem_inc(turn, 1)
            by = bias[:, 0:WIN].rearrange("p (m a r) -> p m a r", a=2, r=NT)
            cut = lambda ap: ap.rearrange("p (m r) -> p m r", r=NT)
            half, m0 = NL // 2, FAR // (2 * NT)
            parts = ((cut(prob[:, u, 0:half]), cut(s_ps[:, 0]), by[:, 0:WROWS // 2, 0]),
                     (cut(prob[:, u, half:NL]), cut(s_ps[:, 1]), by[:, WROWS // 2:, 0]),
                     (cut(prob[:, u, NL:NL + NH]), cut(s_ps[:, 2, 0:NH]), by[:, m0:, 1]),
                     (prob[:, u, NL + NH:], s_ps[:, 2, NH:NH + NT], bias[:, WIN:]))
            for n, (o, sc, bb) in enumerate(parts):
                ins = nc.vector.tensor_tensor_reduce(o, sc, bb, -SCALE, 3e38, ALU.add, ALU.min, mn[:, n:n + 1])
            ins.then_inc(min_done, 1)
            dve.wait_ge(min_done, s + 1)
            nc.vector.tensor_reduce(nm[:, u:u + 1], mn[:], AX, ALU.min).then_inc(nm_done, 1)

        for u in range(2):
            dve.sem_inc(out_free[u], 16 * HA)
        dve.sem_inc(o_done, 2)
        dve.wait_ge(zeroed, 1)
        dve.wait_ge(const, 16 * 3)
        queries(0, 0)
        queries(1, 1)
        dve.wait_ge(bias_landed, 16 * HA)
        scores(0, 0)

        def turn_of(s, i, u, ahead):
            if ahead >= 1:
                scores(s + 1, 1 - u)
            if ahead >= 2:
                queries(s + 2, u)
            dve.wait_ge(e_done, s + 1)
            nc.vector.reciprocal(den[:, u:u + 1], den[:, u:u + 1]).then_inc(r_done, 1)
            dve.wait_ge(r_done, s + 1)
            dve.wait_ge(out_free[u], 16 * HA * (i + 1))
            dve.wait_ge(pv_done, s + 3)
            dve.sem_inc(turn, 1)
            nc.vector.tensor_scalar(out[:, u], o_ps[:, u], den[:, u:u + 1], None, ALU.mult).then_inc(o_done, 1)
        turns(dve, turn_of)

    def scalar(act):
        act.wait_ge(repeated, 32)
        for h in range(HA):
            src = bass.AP(tensor=rep_d.tensor, offset=h * LD + NT - 1, ap=[[HA * LD - 1, NT], [1, WIN + NT]])
            act.dma_start(bias[h * NT:(h + 1) * NT, :], src).then_inc(bias_landed, 16)

        def exponentials(s, u):
            act.wait_ge(nm_done, s + 1)
            nc.scalar.activation(prob[:, u], prob[:, u], ACT.Exp, bias=nm[:, u:u + 1], scale=-1.0,
                                 accum_out=den[:, u:u + 1]).then_inc(e_done, 1)

        def turn_of(s, i, u, ahead):
            act.wait_ge(t_done, s + 3)
            act.wait_ge(pv_done, s + 1)
            for t0, t1 in ((0, 8), (8, NKT - 1), (NKT - 1, NKT)):
                w, c = rows_of[t0], (t0 % 8) * R
                ins = nc.scalar.activation(probT[0:w, u, t0:t1].rearrange("p a k -> p (a k)"),
                                           t_ps[0:w, t0 // 8, c:c + (t1 - t0) * R], ACT.Copy)
            ins.then_inc(pt_done, 1)
            if ahead >= 1:
                exponentials(s + 1, 1 - u)
        exponentials(0, 0)
        turns(act, turn_of)

    def tensor(pe):
        def scores(s, i, u):
            pe.wait_ge(q_done, s + 1)
            pe.wait_ge(k_landed[u], 32 * (i + 1))
            parts = [(s_ps[:, 0], lambda g: klow[:, u, g, 0:512]), (s_ps[:, 1], lambda g: klow[:, u, g, 512:NL]),
                     (s_ps[:, 2, 0:NH], lambda g: khigh[:, u, g]), (s_ps[:, 2, NH:NH + NT], lambda g: kn[:, u, g])]
            for o, keys in parts:
                for g in range(NG):
                    mm = pe.matmul(o, qb[:, g, u], keys(g), start=(g == 0), stop=(g == NG - 1))
            mm.then_inc(qk_done, 1)

        pe.sem_inc(t_done, 2)
        pe.sem_inc(pt_done, 1)
        pe.sem_inc(pv_done, 2)
        pe.wait_ge(const, 16 * 3)
        pe.wait_ge(*bank_read)
        scores(0, 0, 0)

        def turn_of(s, i, u, ahead):
            pe.wait_ge(e_done, s + 1)
            pe.wait_ge(pt_done, s + 1)
            pe.sem_inc(turn_pe, 1)
            for a, cols in enumerate(ktiles):
                mm = pe.transpose(t_ps[0:rows_of[a], a // 8, (a % 8) * R:(a % 8 + 1) * R], prob[:, u, cols],
                                  ident[0:R, 0:R])
            mm.then_inc(t_done, 1)
            if ahead >= 1:
                pe.wait_ge(nm_done, s + 1)
                scores(s + 1, i + u, 1 - u)
            pe.wait_ge(pt_done, s + 2)
            pe.wait_ge(o_done, s + 1)
            pe.wait_ge(v_landed[u], 16 * NVL * (i + 1))
            values = ([vlow[:, u, a] for a in range(NT)] + [vhigh[:, u, a] for a in range(NH // P)] + [vn[:, u]])
            for a, vv in enumerate(values):
                mm = pe.matmul(o_ps[:, u], probT[0:rows_of[a], u, a], vv, start=(a == 0), stop=(a == NKT - 1))
            mm.then_inc(pv_done, 1)
        turns(pe, turn_of)
    return dict(load=load, sync=sync, gpsimd=gpsimd, scalar=scalar, vector=vector, tensor=tensor)


def sample_branches(nc, projT, projN, a, rep_p, rep_d, o_b, attn_s, state_out):
    with ExitStack() as ctx:
        bank = ctx.enter_context(nc.psum_tensor("sample_banks", [P, 7, 512], F32))
        bias = bias_vectors(ctx, nc, bank, a["rel_bias"], a["expand"], rep_p, rep_d)
        hgrn = hgrn_sample(ctx, nc, bank, bias["read"], projT, projN, a["lbT"], a["go_on_s"], a["smask"], a["rowm"],
                           a["ident"], a["state"], o_b, state_out)
        attn = attention_sample(ctx, nc, bank, hgrn["read"], bias["repeated"], projT, projN, a["cache_kT"], a["cache_v"],
                                rep_d, a["ident"], attn_s)
        with nc.Block() as block:
            @block.sync
            def _(sp):
                bias["load"](sp)
                hgrn["load"](sp)
                bias["repeat"](sp)
                attn["load"](sp)
                hgrn["store"](sp)
                attn["sync"](sp)

            @block.gpsimd
            def _(pool):
                hgrn["gpsimd"](pool)
                attn["gpsimd"](pool)

            @block.scalar
            def _(act):
                hgrn["scalar"](act)
                attn["scalar"](act)

            @block.vector
            def _(dve):
                bias["vector"](dve)
                hgrn["vector"](dve)
                attn["vector"](dve)

            @block.tensor
            def _(pe):
                bias["tensor"](pe)
                hgrn["tensor"](pe)
                attn["tensor"](pe)


def merge_and_project(nc, x_all, partials, attn_s, projN, o_b, w_o, norm_g, ln_g, ln_b, ident_d, y):
    NTL = T // P
    H = 512
    with ExitStack() as ctx:
        sb, ps, sem = region(ctx, nc)
        ident = sb("m_ident", [P, P])
        wraw = sb("m_wraw", [P, KD, D])
        whi, wlo = sb("m_whi", [P, KD, D], F32R), sb("m_wlo", [P, KD, D], F32R)
        ngb, lgb, lbb = sb("m_ngb", [P, WB]), sb("m_lgb", [P, D]), sb("m_lbb", [P, D])
        half = sb("m_half", [P, HB])
        xt = sb("m_x", [P, 4, D])
        pt = sb("m_part", [P, 2, NC, HA, OW])
        gate, ob = sb("m_gate", [P, 2, 2, H]), sb("m_ob", [P, 2, H])
        mn, wexp, wd, dsum = sb("m_mn", [P, HA]), sb("m_wexp", [P, NC, HA]), sb("m_wd", [P, NC, HA]), sb("m_dsum", [P, HA])
        mixa = sb("m_mixa", [TS, H])
        sq, ms, rs = sb("m_sq", [P, H]), sb("m_ms", [P, HB]), sb("m_rs", [P, HB])
        mix = sb("m_mix", [P, D])
        mhi, mlo = sb("m_mhi", [P, 2, KD, P], F32R), sb("m_mlo", [P, 2, KD, P], F32R)
        z = sb("m_z", [P, D])
        st, mv, vr, rstd, nb = sb("m_st", [P, 2, 6]), sb("m_mv", [P, 2]), sb("m_vr", [P, 1]), sb("m_rstd", [P, 1]), sb("m_nb", [P, 1])
        yt = sb("m_y", [P, 2, D])
        t_ps, z_ps = ps("m_t_ps", [P, 2, H]), ps("m_z_ps", [P, 2, 2, H])
        const, w_hi, w_lo = sem("m_const"), sem("m_w_hi"), sem("m_w_lo")
        landed, y_free = ([sem(f"m_{n}{u}") for u in range(2)] for n in ("landed", "y_free"))
        w_landed = [sem(f"m_w_landed{k}") for k in range(KD)]
        sq_done, gate_done = sem("m_sq_done"), sem("m_gate_done")
        chain, d_done, wexp_done, ms_done, rs_done, mix_done = (sem(f"m_{n}") for n in ("chain", "d_done", "wexp_done", "ms_done", "rs_done", "mix_done"))
        t_done, mhi_done, mlo_done, z_done, vr_done, rstd_done, nb_done, n_done, y_done, zr = (
            sem(f"m_{n}") for n in ("t_done", "mhi_done", "mlo_done", "z_done", "vr_done", "rstd_done", "nb_done", "n_done", "y_done", "zr"))
        y_mul, turn_dve, turn_sp = sem("m_y_mul"), sem("m_turn_dve"), sem("m_turn_sp")
        half_set = sem("m_half_set")
        x_landed = [sem(f"m_x_landed{w}") for w in range(4)]
        NLD = 4

        def run(eng, step):
            for t in range(4):
                step(t, 0, t, P, P if t >= 1 else 0, P if t >= 2 else 0)
            with eng.Fori(1, NTL // 4) as i:
                for v in range(4):
                    step(4 * i + v, i, v, P, P, P)
            step(NTL, NTL // 4, 0, TS, P, P)
            step(NTL + 1, NTL // 4, 1, 0, TS, P)
            step(NTL + 2, NTL // 4, 2, 0, 0, TS)

        with nc.Block() as block:
            @block.sync
            def _(sp):
                def load(t, u, v, n=P, sample=False):
                    rows = bass.ds(t * P, n)
                    sp.dma_start(xt[0:n, v], x_all[rows, :]).then_inc(x_landed[v], 16)
                    if sample:
                        sp.dma_start(mixa[0:n, :], attn_s).then_inc(landed[u], 16)
                    else:
                        sp.dma_start(pt[0:n, u], partials[:, rows, :, :].rearrange("c p h w -> p c h w")).then_inc(landed[u], 16)
                    sp.dma_start(gate[0:n, u, 0], projN[rows, WA:2 * WA]).then_inc(landed[u], 16)
                    sp.dma_start(gate[0:n, u, 1], projN[rows, 3 * WA:4 * WA]).then_inc(landed[u], 16)
                    sp.dma_start(ob[0:n, u], o_b[rows, :]).then_inc(landed[u], 16)

                def store(t, u, n=P):
                    sp.wait_ge(y_done, t + 1)
                    sp.sem_inc(turn_sp, 1)
                    sp.dma_start(y[bass.ds(t * P, n), :], yt[0:n, u]).then_inc(y_free[u], 16)

                for u in range(2):
                    sp.sem_inc(y_free[u], 16)
                sp.dma_start(ident[:], ident_d).then_inc(const, 16)
                for dst, src in ((lgb[:], ln_g), (lbb[:], ln_b)):
                    sp.dma_start(dst, src[0:1, :].to_broadcast([P, D])).then_inc(const, 16)
                for h in range(HB):
                    sp.dma_start(ngb[:, h * DB:(h + 1) * DB], norm_g[0:1, :].to_broadcast([P, DB])).then_inc(const, 16)
                load(0, 0, 0)
                load(1, 1, 1)
                for k in range(KD):
                    sp.dma_start(wraw[:, k], w_o[:, k, :]).then_inc(w_landed[k], 16)
                def step(t, v, n, sample=False):
                    sp.wait_ge(mix_done, t + 1)
                    if not (isinstance(t, int) and t < 2):
                        sp.sem_inc(turn_sp, 1)
                        sp.wait_ge(zr, t - 1)
                    sp.sem_inc(turn_sp, 1)
                    load(t + 2, v % 2, (v + 2) % 4, n, sample)
                step(0, 0, P)
                step(1, 1, P)
                step(2, 2, P)
                store(0, 0)
                step(3, 3, P)
                store(1, 1)
                with sp.Fori(1, NTL // 4 - 1) as i:
                    for v in range(4):
                        step(4 * i + v, v, P)
                        store(4 * i + v - 2, v % 2)
                for t in range(NTL - 4, NTL - 2):
                    step(t, t % 4, P)
                    store(t - 2, t % 2)
                step(NTL - 2, 2, TS, True)
                store(NTL - 4, 0)
                for t in range(NTL - 3, NTL):
                    store(t, t % 2)
                store(NTL, 0, TS)
                for u in range(2):
                    sp.wait_ge(y_free[u], 16 * (NTL // 2 + 2 - u))

            @block.vector
            def _(dve):
                tt = nc.vector.tensor_tensor
                nc.vector.memset(half[:], -0.5).then_inc(half_set, 1)
                for k in range(KD):
                    dve.wait_ge(w_hi, k + 1)
                    tt(wlo[:, k], wraw[:, k], whi[:, k].bitcast(F32), ALU.subtract).then_inc(w_lo, 1)
                dve.wait_ge(const, 16 * 7)

                CF, CFS, CB = 12, 3, 2

                def step(t, i, v, nf, nm_, nbk):
                    u, turn = v % 2, 2 * i + v // 2
                    sample = nf == TS
                    if isinstance(t, int):
                        base = sum(CF if s < NTL else (CFS if s == NTL else 0) for s in range(t)) + CB * max(t - 2, 0)
                    else:
                        base = (CF + CB) * t - 2 * CB
                    link = [0]

                    def then(ins):
                        link[0] += 1
                        ins.then_inc(chain, 1)
                        dve.wait_ge(chain, base + link[0])

                    if nf:
                        dve.wait_ge(landed[u], 16 * NLD * (turn + 1))
                        r = slice(0, nf)
                        a = mix[r, 0:H]
                        if isinstance(t, int) and t == 0:
                            pass
                        else:
                            dve.wait_ge(t_done, t)
                        if not sample:
                            nmx = pt[r, u, :, :, DA + 1]
                            then(tt(mn[r], nmx[:, 0], nmx[:, 1], ALU.min))
                            then(tt(mn[r], mn[r], nmx[:, 2], ALU.min))
                            tt(wd[r], mn[r].unsqueeze(1).to_broadcast([nf, NC, HA]), nmx, ALU.subtract).then_inc(d_done, 1)
                        o = ob[r, u]
                        if sample:
                            then(tt(a, mixa[r], gate[r, u, 0], ALU.mult))
                        if not sample:
                            dve.wait_ge(wexp_done, t + 1)
                            then(tt(wd[r], wexp[r], pt[r, u, :, :, DA], ALU.mult))
                            then(tt(dsum[r], wd[r, 0], wd[r, 1], ALU.add))
                            then(tt(dsum[r], dsum[r], wd[r, 2], ALU.add))
                            then(nc.vector.reciprocal(dsum[r], dsum[r]))
                            then(tt(wexp[r], wexp[r], dsum[r].unsqueeze(1).to_broadcast([nf, NC, HA]), ALU.mult))
                            po = pt[r, u].rearrange("p c h w -> p (c h) w")[:, :, 0:DA]
                            wv = wexp[r].rearrange("p c h -> p (c h)").unsqueeze(2).to_broadcast([nf, NC * HA, DA])
                            then(tt(po, po, wv, ALU.mult))
                        dve.wait_ge(sq_done, t + 1)
                        then(nc.vector.tensor_reduce(ms[r], sq[r].rearrange("p (h v) -> p h v", h=HB), AX, ALU.add))
                        nc.vector.tensor_scalar(ms[r], ms[r], 1.0 / DB, EPS, ALU.mult, ALU.add).then_inc(ms_done, 1)
                        if not sample:
                            av = a.rearrange("p (h d) -> p h d", h=HA)
                            then(tt(av, pt[r, u, 0, :, 0:DA], pt[r, u, 1, :, 0:DA], ALU.add))
                            then(tt(av, av, pt[r, u, 2, :, 0:DA], ALU.add))
                            tt(a, a, gate[r, u, 0], ALU.mult)
                        bpart = mix[r, H:D]
                        dve.wait_ge(gate_done, t + 1)
                        dve.wait_ge(rs_done, t + 1)
                        then(tt(o.rearrange("p (h v) -> p h v", h=HB), o.rearrange("p (h v) -> p h v", h=HB),
                                rs[r].unsqueeze(2).to_broadcast([nf, HB, DB]), ALU.mult))
                        tt(bpart, o, gate[r, u, 1], ALU.mult).then_inc(mix_done, 1)
                        want = CFS if sample else CF
                        assert link[0] == want, (link[0], want)
                    if nbk:
                        r = slice(0, nbk)
                        dve.wait_ge(x_landed[(v + 2) % 4], 16 * (i + 1 if v >= 2 else i))
                        dve.wait_ge(z_done, t - 1)
                        if not (isinstance(t, int) and t < 3):
                            dve.wait_ge(n_done, t - 2)
                        for g in range(2):
                            c = slice(g * H, (g + 1) * H)
                            ins = nc.vector.scalar_tensor_tensor(z[r, c], xt[r, (v + 2) % 4, c], ALPHA,
                                                                 z_ps[r, u, g], ALU.mult, ALU.add)
                        ins.then_inc(zr, 1)
                        dve.wait_ge(zr, t - 1)
                        for g in range(2):
                            ins = nc.vector.bn_stats(st[r, g], z[r, g * H:(g + 1) * H])
                        then(ins)
                        dve.sem_inc(turn_dve, 1)
                        then(nc.vector.bn_aggr(mv[r], st[r].rearrange("p a b -> p (a b)")))
                        nc.vector.tensor_scalar(vr[r], mv[r, 1:2], EPS, None, ALU.add).then_inc(vr_done, 1)
                    if nf:
                        dve.wait_ge(mhi_done, t + 1)
                        if not (isinstance(t, int) and t < 2):
                            dve.wait_ge(z_done, t - 1)
                        r = slice(0, nf)
                        for g in range(2):
                            k = slice(4 * g, 4 * g + 4)
                            ins = tt(mlo[:, u, k, 0:nf], t_ps[:, g].rearrange("p (k n) -> p k n", k=4)[:, :, 0:nf],
                                     mhi[:, u, k, 0:nf].bitcast(F32), ALU.subtract)
                        ins.then_inc(mlo_done, 1)
                    if nbk:
                        r = slice(0, nbk)
                        dve.wait_ge(rstd_done, t - 1)
                        nc.vector.scalar_tensor_tensor(nb[r], mv[r, 0:1], -1.0, rstd[r], ALU.mult, ALU.mult).then_inc(nb_done, 1)

                run(dve, step)

            @block.scalar
            def _(act):
                for k in range(KD):
                    act.wait_ge(w_landed[k], 16)
                    nc.scalar.activation(whi[:, k], wraw[:, k], ACT.Copy).then_inc(w_hi, 1)

                def step(t, i, v, nf, nm_, nbk):
                    u, turn = v % 2, 2 * i + v // 2
                    if nf:
                        act.wait_ge(landed[u], 16 * NLD * (turn + 1))
                        if not (isinstance(t, int) and t < 1):
                            act.wait_ge(ms_done, t)
                        nc.scalar.activation(sq[0:nf], ob[0:nf, u], ACT.Square).then_inc(sq_done, 1)
                    if nf == P:
                        act.wait_ge(d_done, t + 1)
                        nc.scalar.activation(wexp[:], wd[:], ACT.Exp).then_inc(wexp_done, 1)
                    if nf:
                        act.wait_ge(t_done, t + 1)
                        if not (isinstance(t, int) and t < 2):
                            act.wait_ge(z_done, t - 1)
                        for g in range(2):
                            ins = nc.scalar.activation(mhi[:, u, 4 * g:4 * g + 4, 0:nf],
                                                       t_ps[:, g].rearrange("p (k n) -> p k n", k=4)[:, :, 0:nf], ACT.Copy)
                        ins.then_inc(mhi_done, 1)
                    if nbk:
                        r = slice(0, nbk)
                        act.wait_ge(nb_done, t - 1)
                        act.wait_ge(y_free[u], 16 * turn)
                        nc.scalar.activation(yt[r, u], z[r], ACT.Identity, bias=nb[r, 0:1], scale=rstd[r, 0:1]).then_inc(n_done, 1)
                run(act, step)

            @block.gpsimd
            def _(pool):
                pool.wait_ge(half_set, 1)
                pool.wait_ge(const, 16 * 7)

                def step(t, i, v, nf, nm_, nbk):
                    u, turn = v % 2, 2 * i + v // 2
                    if nf:
                        r = slice(0, nf)
                        pool.wait_ge(landed[u], 16 * NLD * (turn + 1))
                        nc.gpsimd.tensor_tensor(gate[r, u, 1], gate[r, u, 1], ngb[r], ALU.mult).then_inc(gate_done, 1)
                        pool.wait_ge(ms_done, t + 1)
                        nc.gpsimd.tensor_tensor(rs[r], ms[r], half[r], ALU.pow).then_inc(rs_done, 1)
                    if nbk:
                        r = slice(0, nbk)
                        pool.wait_ge(vr_done, t - 1)
                        nc.gpsimd.tensor_tensor(rstd[r], vr[r], half[r, 0:1], ALU.pow).then_inc(rstd_done, 1)
                        pool.wait_ge(n_done, t - 1)
                        nc.gpsimd.tensor_tensor(yt[r, u], yt[r, u], lgb[r], ALU.mult).then_inc(y_mul, 1)
                        pool.wait_ge(y_mul, t - 1)
                        nc.gpsimd.tensor_tensor(yt[r, u], yt[r, u], lbb[r], ALU.add).then_inc(y_done, 1)
                run(pool, step)

            @block.tensor
            def _(pe):
                pe.wait_ge(const, 16 * 7)
                pe.wait_ge(w_lo, KD)

                def step(t, i, v, nf, nm_, nbk):
                    u, turn = v % 2, 2 * i + v // 2
                    if nf:
                        pe.wait_ge(mix_done, t + 1)
                        if not (isinstance(t, int) and t < 1):
                            pe.wait_ge(mlo_done, t)
                        for k in range(KD):
                            mm = pe.transpose(t_ps[:, k // 4, (k % 4) * P:(k % 4) * P + nf], mix[0:nf, k * P:(k + 1) * P],
                                              ident[0:nf, 0:nf])
                        mm.then_inc(t_done, 1)
                    if nm_:
                        w = 1 - u
                        pe.wait_ge(mlo_done, t)
                        if not (isinstance(t, int) and t < 3):
                            pe.wait_ge(zr, t - 2)
                        for k in range(KD):
                            for a, (m, ww) in enumerate(((mhi, whi), (mhi, wlo), (mlo, whi))):
                                for g in range(2):
                                    mm = pe.matmul(z_ps[0:nm_, w, g], m[:, w, k, 0:nm_], ww[:, k, g * H:(g + 1) * H],
                                                   start=(k == 0 and a == 0), stop=(k == KD - 1 and a == 2))
                        mm.then_inc(z_done, 1)
                run(pe, step)


def build(nc, a, o):
    dram = lambda name, shape: nc.dram_tensor(name, shape, F32, kind="Internal").ap()
    projT = dram("projT", [NCT, P, TT])
    projN = dram("projN", [TT, WN])
    win = (o["kwin_s"], a["cache_kT"], o["vwin_s"], a["cache_v"])
    project_transposed(nc, a["xT"], a["w_t"], projT)
    project_natural(nc, a["xT"], a["w_n"], projT, projN, o["kwin_p"], o["vwin_p"], o["kwin_s"], o["vwin_s"])
    rep_p, rep_d = dram("rep_p", [P, HA, NC * LB]), dram("rep_d", [NT, HA, LD])
    o_b = dram("o_b", [TT, WB])
    attn_s = dram("attn_s", [TS, WA])
    sample_branches(nc, projT, projN, a, rep_p, rep_d, o_b, attn_s, o["hgrn_s"])
    hgrn_prompt(nc, projT, projN, a["lbT"], a["go_on"], a["lmask"], a["dmask"], a["ident"], o_b, o["hgrn_p"], win)
    partials = dram("partials", [NC, T, HA, OW])
    attention_prompt(nc, projT, projN, rep_p, a["ident"], partials, win)
    merge_and_project(nc, a["x"], partials, attn_s, projN, o_b, a["w_o"], a["norm_g"], a["ln_g"], a["ln_b"], a["ident"], o["y"])


def kernel(x_prompt, x_sample, cache_k, cache_v, state_hgrn, w_in, w_out, rel_bias, lb_param, hgrn_norm_g,
           ln_g, ln_b):
    import concourse.bacc as bacc
    from concourse.bass_utils import run_bass_kernel_spmd

    A = np.asarray
    x_all = np.concatenate([A(x_prompt).reshape(T, D), A(x_sample).reshape(TS, D)])
    w = A(w_in)[0].reshape(KD, P, 8, 512)
    arrays = {
        "x": x_all,
        "xT": x_all.T.reshape(KD, P, TT).transpose(1, 0, 2),
        "w_t": w[:, :, [0, 1, 4, 5]].reshape(KD, P, NCT, P).transpose(2, 1, 0, 3),
        "w_n": w[:, :, [2, 3, 6, 7]].reshape(KD, P, WN).transpose(1, 0, 2),
        "cache_kT": A(cache_k)[0].reshape(NB, WROWS, 2, NT, WA).transpose(0, 4, 2, 1, 3),
        "cache_v": A(cache_v)[0].reshape(NB, WIN, WA),
        "state": A(state_hgrn)[0],
        "w_o": A(w_out)[0].reshape(KD, P, D).transpose(1, 0, 2),
        "rel_bias": A(rel_bias),
        "lbT": A(lb_param).reshape(2, HB, P).transpose(2, 0, 1),
        "norm_g": A(hgrn_norm_g), "ln_g": A(ln_g), "ln_b": A(ln_b),
        **shape_constants(),
    }
    outs = {
        "y": [TT, D], "kwin_p": [NG, P, T], "vwin_p": [T, WA],
        "kwin_s": [NB, WA, 2, WROWS, NT], "vwin_s": [NB, WIN, WA],
        "hgrn_p": [HB, DB, DB], "hgrn_s": [NB, HB, DB, DB],
    }
    nc = bacc.Bacc("TRN2", target_bir_lowering=False, num_devices=1)
    arrays = {f"in_{k}": np.ascontiguousarray(v) for k, v in arrays.items()}
    ins = {k[3:]: nc.dram_tensor(k, v.shape, mybir.dt.from_np(v.dtype), kind="ExternalInput").ap()
           for k, v in arrays.items()}
    outp = {k: nc.dram_tensor(f"out_{k}", s, F32, kind="ExternalOutput").ap() for k, s in outs.items()}
    build(nc, ins, outp)
    r = run_bass_kernel_spmd(nc, [arrays], core_ids=[0]).results[0]
    g = {k: r[f"out_{k}"] for k in outs}
    return (g["y"][:T].reshape(1, T, D), g["y"][T:].reshape(NB, NT, D),
            g["kwin_p"].reshape(1, 1, HA, DA, T).transpose(0, 1, 4, 2, 3), g["vwin_p"].reshape(1, 1, T, HA, DA),
            g["kwin_s"].transpose(0, 3, 2, 4, 1).reshape(1, NB, WIN, HA, DA),
            g["vwin_s"].reshape(1, NB, WIN, HA, DA),
            g["hgrn_p"].reshape(1, 1, HB, DB, DB), g["hgrn_s"].reshape(1, NB, HB, DB, DB))
```
